# Optimizing a Trainium2 kernel written in Bass

```python
import jax, jax.numpy as jnp
from jax import lax
import numpy as np

D_MODEL = 1024
BATCH = 1
SEQ = 512
DEPTH = 1

N_META = 16
GRID_W = 64
NA_WIN_ROWS = 8
NA_WIN_COLS = 16
NA_HEADS = 8
NA_HEAD_DIM = 64
NA_WIDTH = NA_HEADS * NA_HEAD_DIM
GLA_HEADS = 4
GLA_DK = 64
GLA_DV = 128
GLA_KW = GLA_HEADS * GLA_DK
GLA_VW = GLA_HEADS * GLA_DV
GLA_GATE_RANK = 16
GLA_GATE_TAU = 16.0
GLA_CHUNK = 64
MIX_WIDTH = NA_WIDTH + GLA_VW
IN_COLS = 3 * NA_WIDTH + 2 * GLA_KW + 2 * GLA_VW + 2 * GLA_GATE_RANK
D_FF = 2816
CONV_W = 3
RMS_EPS = 1e-6


def rmsnorm(x, g):
    xf = x.astype(jnp.float32)
    y = xf * lax.rsqrt(jnp.mean(xf * xf, axis=-1, keepdims=True) + RMS_EPS)
    return (y * g.astype(jnp.float32)).astype(x.dtype)

def neighbourhood_attention(q, k, v, rpb):
    B, L, H, dh = q.shape
    T = L - N_META
    W = GRID_W
    R = T // W
    kh = min(NA_WIN_ROWS, R)
    kw = NA_WIN_COLS
    q = q * (dh ** -0.5)
    qm, km, vm = q[:, :N_META], k[:, :N_META], v[:, :N_META]

    def grid(t):
        return t[:, N_META:].reshape(B, R, W, H, dh).transpose(0, 3, 1, 2, 4)

    qg, kg, vg = grid(q), grid(k), grid(v)
    rs = jnp.clip(jnp.arange(R) - kh // 2, 0, R - kh)
    row_idx = rs[:, None] + jnp.arange(kh)[None, :]
    k_rows = kg[:, :, row_idx]
    v_rows = vg[:, :, row_idx]
    cq = jnp.arange(W)
    cs = jnp.clip(cq - kw // 2, 0, W - kw)
    in_win = (cq[None, :] >= cs[:, None]) & (cq[None, :] < cs[:, None] + kw)
    dr = row_idx - jnp.arange(R)[:, None] + (NA_WIN_ROWS - 1)
    dc = jnp.clip(cq[None, :] - cq[:, None], -(kw - 1), kw - 1) + (NA_WIN_COLS - 1)
    bias = rpb[:, dr[:, None, :, None], dc[None, :, None, :]]

    s_loc = jnp.einsum('bhrcd,bhrikd->bhrcik', qg, k_rows).astype(jnp.float32) + bias.astype(jnp.float32)
    s_loc = jnp.where(in_win[:, None, :], s_loc, -jnp.inf)
    s_meta = jnp.einsum('bhrcd,bmhd->bhrcm', qg, km).astype(jnp.float32)
    s_all = jnp.concatenate([s_loc.reshape(B, H, R, W, kh * W), s_meta], axis=-1)
    p = jax.nn.softmax(s_all, axis=-1).astype(v.dtype)
    p_loc = p[..., :kh * W].reshape(B, H, R, W, kh, W)
    p_meta = p[..., kh * W:]
    og = (jnp.einsum('bhrcik,bhrikd->bhrcd', p_loc, v_rows)
          + jnp.einsum('bhrcm,bmhd->bhrcd', p_meta, vm))
    og = og.transpose(0, 2, 3, 1, 4).reshape(B, T, H * dh)
    sm = jnp.einsum('bqhd,bkhd->bhqk', qm, km).astype(jnp.float32)
    pm = jax.nn.softmax(sm, axis=-1).astype(v.dtype)
    om = jnp.einsum('bhqk,bkhd->bqhd', pm, vm).reshape(B, N_META, H * dh)
    return jnp.concatenate([om, og], axis=1)

def gla_chunked(q, k, v, log_a, strict):
    C = q.shape[-2]
    b = jnp.cumsum(log_a, axis=-2)
    b_last = b[..., -1:, :]
    q_dec = q * jnp.exp(b)
    k_inv = k * jnp.exp(-b)
    k_end = k * jnp.exp(b_last - b)
    mask = jnp.tril(jnp.ones((C, C), dtype=bool), k=-1 if strict else 0)
    a = jnp.where(mask, jnp.einsum('bhncd,bhnsd->bhncs', q_dec, k_inv), 0.0)
    o = jnp.einsum('bhncs,bhnse->bhnce', a, v)
    ds = jnp.einsum('bhncd,bhnce->nbhde', k_end, v)
    decay = jnp.exp(b_last[..., 0, :]).transpose(2, 0, 1, 3)

    def step(s, inp):
        dec, d = inp
        return dec[..., None] * s + d, s

    s0 = jnp.zeros(ds.shape[1:], ds.dtype)
    _, s_prev = lax.scan(step, s0, (decay, ds))
    return o + jnp.einsum('bhncd,nbhde->bhnce', q_dec, s_prev)

def gla_bidirectional(q, k, v, g, z, up_f, bias_f, up_b, bias_b, out_gain):
    B, L, _ = q.shape
    H, dk, dv, C = GLA_HEADS, GLA_DK, GLA_DV, GLA_CHUNK
    f32 = jnp.float32
    pad = (-N_META) % C
    Lp = L + pad
    N = Lp // C
    la_f = jax.nn.log_sigmoid((z[..., :GLA_GATE_RANK] @ up_f + bias_f).astype(f32)) / GLA_GATE_TAU
    la_b = jax.nn.log_sigmoid((z[..., GLA_GATE_RANK:] @ up_b + bias_b).astype(f32)) / GLA_GATE_TAU

    def pad_seq(t, d):
        return jnp.pad(t.astype(f32).reshape(B, L, H, d), ((0, 0), (pad, 0), (0, 0), (0, 0)))

    def chunk(t):
        return t.reshape(B, N, C, H, t.shape[-1]).transpose(0, 3, 1, 2, 4)

    def unchunk(t):
        return t.transpose(0, 2, 3, 1, 4).reshape(B, Lp, H, t.shape[-1])

    qp = pad_seq(q * (dk ** -0.5), dk)
    kp = pad_seq(k, dk)
    vp = pad_seq(v, dv)
    lfp = pad_seq(la_f, dk)
    lbp = pad_seq(la_b, dk)
    o_f = unchunk(gla_chunked(chunk(qp), chunk(kp), chunk(vp), chunk(lfp), False))
    rev = lambda t: t[:, ::-1]
    o_b = rev(unchunk(gla_chunked(chunk(rev(qp)), chunk(rev(kp)), chunk(rev(vp)), chunk(rev(lbp)), True)))
    o = (o_f + o_b)[:, pad:].astype(q.dtype)
    o = rmsnorm(o, out_gain) * jax.nn.silu(g.reshape(B, L, H, dv))
    return o.reshape(B, L, H * dv)

def hybrid_layer(h, norm_mix_pre, w_in, rpb, na_gain, up_f, bias_f, up_b, bias_b, gla_gain,
                 w_o, norm_mix_post, norm_ffn_pre, w_ffn_in, conv_w, conv_b, w_ffn_out, norm_ffn_post):
    B, L, _ = h.shape
    u = rmsnorm(h, norm_mix_pre)
    proj = u @ w_in
    sizes = [NA_WIDTH, NA_WIDTH, NA_WIDTH, GLA_KW, GLA_KW, GLA_VW, GLA_VW, 2 * GLA_GATE_RANK]
    offs = np.cumsum([0] + sizes)
    parts = [proj[..., int(offs[i]):int(offs[i + 1])] for i in range(len(sizes))]
    q_na, k_na, v_na, q_gl, k_gl, v_gl, g_gl, z_gl = parts
    shp = (B, L, NA_HEADS, NA_HEAD_DIM)
    o_na = neighbourhood_attention(q_na.reshape(shp), k_na.reshape(shp), v_na.reshape(shp), rpb)
    o_na = rmsnorm(o_na, na_gain)
    o_gl = gla_bidirectional(q_gl, k_gl, v_gl, g_gl, z_gl, up_f, bias_f, up_b, bias_b, gla_gain)
    mix = jnp.concatenate([o_na, o_gl], axis=-1) @ w_o
    h = h + rmsnorm(mix, norm_mix_post)
    a = rmsnorm(h, norm_ffn_pre) @ w_ffn_in
    half = CONV_W // 2
    ap = jnp.pad(a, ((0, 0), (half, half), (0, 0)))
    a = sum(ap[:, j:j + L] * conv_w[j] for j in range(CONV_W)) + conv_b
    val, gate = a[..., :D_FF], a[..., D_FF:]
    y = (jax.nn.gelu(gate, approximate=True) * val) @ w_ffn_out
    return h + rmsnorm(y, norm_ffn_post)

def first_inputs(seed: int = 0) -> dict:
    key = jax.random.key(seed)
    ks = jax.random.split(key, 20)
    f32 = jnp.float32

    def nrm(k, shape, scale):
        return jax.random.normal(k, shape, f32) * scale

    def gain(k, shape):
        return 1.0 + 0.1 * jax.random.normal(k, shape, f32)

    return {
        'x': nrm(ks[0], (BATCH, SEQ, D_MODEL), 1.0),
        'meta_tokens': nrm(ks[1], (N_META, D_MODEL), 1.0),
        'norm_mix_pre': gain(ks[2], (DEPTH, D_MODEL)),
        'w_in': nrm(ks[3], (DEPTH, D_MODEL, IN_COLS), D_MODEL ** -0.5),
        'na_rel_bias': nrm(ks[4], (DEPTH, NA_HEADS, 2 * NA_WIN_ROWS - 1, 2 * NA_WIN_COLS - 1), 0.5),
        'na_out_gain': gain(ks[5], (DEPTH, NA_WIDTH)),
        'gla_gate_up_fwd': nrm(ks[6], (DEPTH, GLA_GATE_RANK, GLA_KW), GLA_GATE_RANK ** -0.5),
        'gla_gate_bias_fwd': nrm(ks[7], (DEPTH, GLA_KW), 0.5),
        'gla_gate_up_bwd': nrm(ks[8], (DEPTH, GLA_GATE_RANK, GLA_KW), GLA_GATE_RANK ** -0.5),
        'gla_gate_bias_bwd': nrm(ks[9], (DEPTH, GLA_KW), 0.5),
        'gla_out_gain': gain(ks[10], (DEPTH, GLA_DV)),
        'w_o': nrm(ks[11], (DEPTH, MIX_WIDTH, D_MODEL), MIX_WIDTH ** -0.5),
        'norm_mix_post': gain(ks[12], (DEPTH, D_MODEL)),
        'norm_ffn_pre': gain(ks[13], (DEPTH, D_MODEL)),
        'w_ffn_in': nrm(ks[14], (DEPTH, D_MODEL, 2 * D_FF), D_MODEL ** -0.5),
        'ffn_conv_w': nrm(ks[15], (DEPTH, CONV_W, 2 * D_FF), CONV_W ** -0.5),
        'ffn_conv_b': nrm(ks[16], (DEPTH, 2 * D_FF), 0.02),
        'w_ffn_out': nrm(ks[17], (DEPTH, D_FF, D_MODEL), D_FF ** -0.5),
        'norm_ffn_post': gain(ks[18], (DEPTH, D_MODEL)),
    }

def first_block(x, meta_tokens, norm_mix_pre, w_in, na_rel_bias, na_out_gain, gla_gate_up_fwd,
              gla_gate_bias_fwd, gla_gate_up_bwd, gla_gate_bias_bwd, gla_out_gain, w_o, norm_mix_post,
              norm_ffn_pre, w_ffn_in, ffn_conv_w, ffn_conv_b, w_ffn_out, norm_ffn_post):
    B = x.shape[0]
    meta = jnp.broadcast_to(meta_tokens.astype(x.dtype)[None], (B, N_META, x.shape[-1]))
    h = jnp.concatenate([meta, x], axis=1)
    for l in range(DEPTH):
        h = hybrid_layer(h, norm_mix_pre[l], w_in[l], na_rel_bias[l], na_out_gain[l],
                         gla_gate_up_fwd[l], gla_gate_bias_fwd[l], gla_gate_up_bwd[l], gla_gate_bias_bwd[l],
                         gla_out_gain[l], w_o[l], norm_mix_post[l], norm_ffn_pre[l], w_ffn_in[l],
                         ffn_conv_w[l], ffn_conv_b[l], w_ffn_out[l], norm_ffn_post[l])
    return h[:, N_META:]


HEAD_DIM = 64
ATTN_Q_HEADS = D_MODEL // (2 * HEAD_DIM)
ATTN_KV_HEADS = ATTN_Q_HEADS // 4
ATTN_GROUP = ATTN_Q_HEADS // ATTN_KV_HEADS
ATTN_WIDTH = ATTN_Q_HEADS * HEAD_DIM
KV_WIDTH = ATTN_KV_HEADS * HEAD_DIM
WINDOW = 128
BLOCK = 128
ROPE_THETA = 500000.0
ROT_DIM = HEAD_DIM // 4
RWKV_HEADS = D_MODEL // (2 * HEAD_DIM)
RWKV_WIDTH = RWKV_HEADS * HEAD_DIM
DECAY_RANK = 64
ICLR_RANK = 64
GATE_RANK = 128
N_BRANCH = 2
D_FF_2 = 4 * D_MODEL
PLE_DIM = 256
NORM_EPS = 1e-6
GN_EPS = 64e-5
O_Q = 0
O_K = O_Q + ATTN_WIDTH
O_V = O_K + KV_WIDTH
O_RWKV = O_V + KV_WIDTH
RWKV_COLS = 3 * RWKV_WIDTH + DECAY_RANK + ICLR_RANK + GATE_RANK
O_GATE = O_RWKV + RWKV_COLS
IN_COLS_2 = O_GATE + N_BRANCH * D_MODEL


def rms_norm(x, g):
    xf = x.astype(jnp.float32)
    y = xf * lax.rsqrt(jnp.mean(xf * xf, axis=-1, keepdims=True) + NORM_EPS)
    return (y * g.astype(jnp.float32)).astype(x.dtype)

def rotary_partial(x, positions):
    half = ROT_DIM // 2
    inv_freq = jnp.power(jnp.float32(ROPE_THETA), -jnp.arange(half, dtype=jnp.float32) * 2.0 / ROT_DIM)
    ang = positions.astype(jnp.float32)[:, None] * inv_freq[None, :]
    cos = jnp.cos(ang)[None, :, None, :]
    sin = jnp.sin(ang)[None, :, None, :]
    xf = x[..., :ROT_DIM].astype(jnp.float32)
    x1, x2 = xf[..., :half], xf[..., half:]
    rot = jnp.concatenate([x1 * cos - x2 * sin, x2 * cos + x1 * sin], axis=-1).astype(x.dtype)
    return jnp.concatenate([rot, x[..., ROT_DIM:]], axis=-1)

def band_windows(t, n_blocks):
    b, _, h, d = t.shape
    tp = jnp.pad(t, ((0, 0), (BLOCK, BLOCK), (0, 0), (0, 0))).reshape(b, n_blocks + 2, BLOCK, h, d)
    return jnp.concatenate([tp[:, :-2], tp[:, 1:-1], tp[:, 2:]], axis=2)

def windowed_gqa(q, k, v, sink):
    b, s = q.shape[0], q.shape[1]
    nb = s // BLOCK
    qb = q.reshape(b, nb, BLOCK, ATTN_KV_HEADS, ATTN_GROUP, HEAD_DIM)
    kw = band_windows(k, nb)
    vw = band_windows(v, nb)
    scores = jnp.einsum('bnqhgd,bnkhd->bnhgqk', qb, kw).astype(jnp.float32) * (HEAD_DIM ** -0.5)
    qpos = jnp.arange(nb)[:, None] * BLOCK + jnp.arange(BLOCK)[None, :]
    kpos = (jnp.arange(nb)[:, None] - 1) * BLOCK + jnp.arange(3 * BLOCK)[None, :]
    valid = ((jnp.abs(qpos[:, :, None] - kpos[:, None, :]) <= WINDOW)
             & (kpos[:, None, :] >= 0) & (kpos[:, None, :] < s))
    scores = jnp.where(valid[None, :, None, None], scores, -1e30)
    sink_logit = jnp.broadcast_to(
        sink.astype(jnp.float32).reshape(ATTN_KV_HEADS, ATTN_GROUP)[None, None, :, :, None, None],
        scores.shape[:-1] + (1,))
    probs = jax.nn.softmax(jnp.concatenate([scores, sink_logit], axis=-1), axis=-1)[..., :-1]
    out = jnp.einsum('bnhgqk,bnkhd->bnqhgd', probs.astype(v.dtype), vw)
    return out.reshape(b, s, ATTN_WIDTH)

def centred_shift(z):
    prev = jnp.pad(z[:, :-1], ((0, 0), (1, 0), (0, 0)))
    nxt = jnp.pad(z[:, 1:], ((0, 0), (0, 1), (0, 0)))
    return 0.5 * (prev + nxt)

def rwkv7_bidir_scan(r, w, k, v, a, b):
    xs = (jnp.moveaxis(r, 2, 0), jnp.moveaxis(w, 2, 0), jnp.moveaxis(k, 2, 0),
          jnp.moveaxis(v, 2, 0), jnp.moveaxis(a, 2, 0), jnp.moveaxis(b, 2, 0))

    def step(state, inp):
        r_t, w_t, k_t, v_t, a_t, b_t = inp
        sa = jnp.einsum('dbhij,dbhj->dbhi', state, a_t)
        state = (state * w_t[..., None, :] + sa[..., :, None] * b_t[..., None, :]
                 + v_t[..., :, None] * k_t[..., None, :])
        y = jnp.einsum('dbhij,dbhj->dbhi', state, r_t)
        return state, y

    d, bsz, _, h, n = r.shape
    s0 = jnp.zeros((d, bsz, h, n, n), jnp.float32)
    _, ys = lax.scan(step, s0, xs)
    return jnp.moveaxis(ys, 0, 2)

def rwkv7_time_mix(z, w0, w2, a0, a2, g2, k_k, k_a, r_k, lnx_w, lnx_b):
    f32 = jnp.float32
    bsz, t = z.shape[0], z.shape[1]
    c = RWKV_WIDTH
    hn = (RWKV_HEADS, HEAD_DIM)
    r = z[..., :c]
    k = z[..., c:2 * c]
    v = z[..., 2 * c:3 * c]
    o = 3 * c
    wl = z[..., o:o + DECAY_RANK]
    o += DECAY_RANK
    al = z[..., o:o + ICLR_RANK]
    o += ICLR_RANK
    gl = z[..., o:o + GATE_RANK]
    w_raw = (w0[:, None, None, :] + jnp.einsum('btr,drc->dbtc', jnp.tanh(wl), w2)).astype(f32)
    decay = jnp.exp(-jnp.exp(-jax.nn.softplus(-w_raw) - 0.5))
    a = jax.nn.sigmoid((a0[:, None, None, :] + jnp.einsum('btr,drc->dbtc', al, a2)).astype(f32))
    g = (jax.nn.sigmoid(gl) @ g2).astype(f32)
    kk = (k * k_k).astype(f32).reshape(bsz, t, *hn)
    kk = kk / jnp.maximum(jnp.sqrt(jnp.sum(kk * kk, axis=-1, keepdims=True)), 1e-12)
    k_dir = (k.astype(f32)[None] * (1.0 + (a - 1.0) * k_a.astype(f32))).reshape(2, bsz, t, *hn)
    a_h = a.reshape(2, bsz, t, *hn)
    rh = r.astype(f32).reshape(bsz, t, *hn)
    vh = v.astype(f32).reshape(bsz, t, *hn)

    def orient(u):
        return jnp.stack([u[0], jnp.flip(u[1], axis=1)])

    def both(u):
        return jnp.stack([u, jnp.flip(u, axis=1)])

    ys = rwkv7_bidir_scan(both(rh), orient(decay.reshape(2, bsz, t, *hn)), orient(k_dir),
                          both(vh), both(-kk), orient(kk[None] * a_h))
    y = ys[0] + jnp.flip(ys[1], axis=1)
    mu = jnp.mean(y, axis=-1, keepdims=True)
    var = jnp.mean(jnp.square(y - mu), axis=-1, keepdims=True)
    y = ((y - mu) * lax.rsqrt(var + GN_EPS)).reshape(bsz, t, c) * lnx_w.astype(f32) + lnx_b.astype(f32)
    bonus = jnp.einsum('bthn,dbthn,dhn->bth', rh, k_dir, r_k.astype(f32))[..., None] * vh
    out = (y + bonus.reshape(bsz, t, c)) * g
    return out.astype(z.dtype)

def second_inputs(seed: int = 0) -> dict:
    key = jax.random.key(seed)
    ks = jax.random.split(key, 32)
    f32 = jnp.float32
    L = DEPTH

    def nrm(k, shape, scale):
        return jax.random.normal(k, shape, f32) * scale

    def gain(k, shape):
        return 1.0 + 0.05 * jax.random.normal(k, shape, f32)

    return {
        'x': nrm(ks[0], (BATCH, SEQ, D_MODEL), 1.0),
        'p': nrm(ks[1], (DEPTH, BATCH, SEQ, PLE_DIM), 1.0),
        'norm_mix': gain(ks[2], (L, D_MODEL)),
        'w_in': nrm(ks[3], (L, D_MODEL, IN_COLS_2), D_MODEL ** -0.5),
        'shift_mu': jax.random.uniform(ks[4], (L, RWKV_COLS), f32),
        'q_norm': gain(ks[5], (L, HEAD_DIM)),
        'k_norm': gain(ks[6], (L, HEAD_DIM)),
        'sink': nrm(ks[7], (L, ATTN_Q_HEADS), 0.5),
        'w0': jax.random.uniform(ks[8], (L, 2, RWKV_WIDTH), f32, minval=-6.0, maxval=1.0),
        'w2': nrm(ks[9], (L, 2, DECAY_RANK, RWKV_WIDTH), 0.1),
        'a0': nrm(ks[10], (L, 2, RWKV_WIDTH), 0.5),
        'a2': nrm(ks[11], (L, 2, ICLR_RANK, RWKV_WIDTH), ICLR_RANK ** -0.5),
        'g2': nrm(ks[12], (L, GATE_RANK, RWKV_WIDTH), GATE_RANK ** -0.5),
        'k_k': 0.85 + 0.05 * jax.random.normal(ks[13], (L, RWKV_WIDTH), f32),
        'k_a': gain(ks[14], (L, RWKV_WIDTH)),
        'r_k': nrm(ks[15], (L, 2, RWKV_HEADS, HEAD_DIM), 0.1),
        'lnx_w': gain(ks[16], (L, RWKV_WIDTH)),
        'lnx_b': nrm(ks[17], (L, RWKV_WIDTH), 0.02),
        'w_up_attn': nrm(ks[18], (L, ATTN_WIDTH, D_MODEL), ATTN_WIDTH ** -0.5),
        'w_up_rwkv': nrm(ks[19], (L, RWKV_WIDTH, D_MODEL), RWKV_WIDTH ** -0.5),
        'w_out': nrm(ks[20], (L, D_MODEL, D_MODEL), D_MODEL ** -0.5),
        'norm_ffn': gain(ks[21], (L, D_MODEL)),
        'w_ff1': nrm(ks[22], (L, D_MODEL, D_FF_2), D_MODEL ** -0.5),
        'w_ff2': nrm(ks[23], (L, D_FF_2, D_MODEL), D_FF_2 ** -0.5),
        'norm_ple': gain(ks[24], (L, D_MODEL)),
        'w_ple_gate': nrm(ks[25], (L, D_MODEL, D_MODEL), D_MODEL ** -0.5),
        'w_ple': nrm(ks[26], (L, PLE_DIM, D_MODEL), PLE_DIM ** -0.5),
    }

def second_block(x, p, norm_mix, w_in, shift_mu, q_norm, k_norm, sink, w0, w2, a0, a2, g2,
              k_k, k_a, r_k, lnx_w, lnx_b, w_up_attn, w_up_rwkv, w_out, norm_ffn,
              w_ff1, w_ff2, norm_ple, w_ple_gate, w_ple):
    bsz, s = x.shape[0], x.shape[1]
    positions = jnp.arange(s)
    for i in range(DEPTH):
        h = rms_norm(x, norm_mix[i])
        proj = h @ w_in[i]
        q = proj[..., O_Q:O_K].reshape(bsz, s, ATTN_Q_HEADS, HEAD_DIM)
        k = proj[..., O_K:O_V].reshape(bsz, s, ATTN_KV_HEADS, HEAD_DIM)
        v = proj[..., O_V:O_RWKV].reshape(bsz, s, ATTN_KV_HEADS, HEAD_DIM)
        q = rotary_partial(rms_norm(q, q_norm[i]), positions)
        k = rotary_partial(rms_norm(k, k_norm[i]), positions)
        attn = windowed_gqa(q, k, v, sink[i])
        zr = proj[..., O_RWKV:O_GATE]
        zr = zr + shift_mu[i] * (centred_shift(zr) - zr)
        rw = rwkv7_time_mix(zr, w0[i], w2[i], a0[i], a2[i], g2[i], k_k[i], k_a[i],
                            r_k[i], lnx_w[i], lnx_b[i])
        gates = jax.nn.sigmoid(proj[..., O_GATE:].reshape(bsz, s, N_BRANCH, D_MODEL))
        merged = gates[..., 0, :] * (attn @ w_up_attn[i]) + gates[..., 1, :] * (rw @ w_up_rwkv[i])
        x = x + merged @ w_out[i]
        hf = rms_norm(x, norm_ffn[i])
        x = x + jnp.square(jax.nn.relu(hf @ w_ff1[i])) @ w_ff2[i]
        hp = rms_norm(x, norm_ple[i])
        x = x + (p[i] @ w_ple[i]) * jax.nn.sigmoid(hp @ w_ple_gate[i])
    return x


def setup_inputs(seed=0):
    out = dict(first_inputs(seed))
    for name, value in second_inputs(seed + 1).items():
        if name != "x":
            out[name + "_2"] = value
    return out


def reference(
    x, meta_tokens, norm_mix_pre, w_in, na_rel_bias, na_out_gain, gla_gate_up_fwd,
    gla_gate_bias_fwd, gla_gate_up_bwd, gla_gate_bias_bwd, gla_out_gain, w_o, norm_mix_post,
    norm_ffn_pre, w_ffn_in, ffn_conv_w, ffn_conv_b, w_ffn_out, norm_ffn_post, p_2, norm_mix_2,
    w_in_2, shift_mu_2, q_norm_2, k_norm_2, sink_2, w0_2, w2_2, a0_2, a2_2, g2_2, k_k_2, k_a_2,
    r_k_2, lnx_w_2, lnx_b_2, w_up_attn_2, w_up_rwkv_2, w_out_2, norm_ffn_2, w_ff1_2, w_ff2_2,
    norm_ple_2, w_ple_gate_2, w_ple_2,
):
    x = first_block(
        x, meta_tokens, norm_mix_pre, w_in, na_rel_bias, na_out_gain, gla_gate_up_fwd,
        gla_gate_bias_fwd, gla_gate_up_bwd, gla_gate_bias_bwd, gla_out_gain, w_o, norm_mix_post,
        norm_ffn_pre, w_ffn_in, ffn_conv_w, ffn_conv_b, w_ffn_out, norm_ffn_post,
    )
    return second_block(
        x, p_2, norm_mix_2, w_in_2, shift_mu_2, q_norm_2, k_norm_2, sink_2, w0_2, w2_2, a0_2,
        a2_2, g2_2, k_k_2, k_a_2, r_k_2, lnx_w_2, lnx_b_2, w_up_attn_2, w_up_rwkv_2, w_out_2,
        norm_ffn_2, w_ff1_2, w_ff2_2, norm_ple_2, w_ple_gate_2, w_ple_2,
    )


_drawn_inputs = setup_inputs


def setup_inputs(seed=0):
    import zlib

    import numpy as np

    out = dict(_drawn_inputs(seed))
    spreads = {}
    factors = {'ffn_conv_b': 3.225,
     'norm_mix_2': 3.439,
     'q_norm_2': 8.0,
     'k_norm_2': 8.0,
     'sink_2': 8.0,
     'w2_2': 6.412,
     'k_k_2': 38.4,
     'k_a_2': 4.629,
     'lnx_w_2': 43.816,
     'lnx_b_2': 64.0,
     'norm_ple_2': 200.0,
     'norm_ffn_2': 8.0,
     'p_2': 6.623,
     'w_ple_gate_2': 8.0,
     'w_ple_2': 6.61}
    for name, (base, spread) in spreads.items():
        noise = np.random.default_rng([zlib.crc32(name.encode()), seed]).standard_normal(out[name].shape)
        drawn = base * np.exp(spread * noise) if base else spread * noise
        out[name] = __import__('jax').numpy.asarray(drawn.astype(out[name].dtype))
    for name, factor in factors.items():
        out[name] = (out[name] * factor).astype(out[name].dtype)
    return out
```

```python
import numpy as np
import concourse.bass as bass
from concourse import mybir
from contextlib import ExitStack

F32 = mybir.dt.float32
F32R = mybir.dt.float32r
U8 = mybir.dt.uint8
ALU = mybir.AluOpType
ACT = mybir.ActivationFunctionType
X = mybir.AxisListType.X

P = 128
D = 1024
KT = D // P
META = 16
GRID = 512
L = META + GRID
HALF = L // 2
SLOT = 256
EPS = 1e-6
NA_H, NA_D = 8, 64
NA_ROWS, NA_COLS = 8, 64
WIN = 16
RPB_R, RPB_C = 15, 31
PAD_C = RPB_C + 2 * 48
GLA_H, GLA_DK, GLA_DV = 4, 64, 128
CH = 64
DFF = 2816
FT = DFF // P
D_FF2 = 4096
HD = 64
NB = GRID // P
WINDOW = 128
ROT = 8
RW_FI = 4
NCH = GRID // CH
GN_EPS = 64e-5
NEG = -1e30

PARAMS = {}
_at = 0
for _name, _n in (("mix_pre", 8), ("na_gain", 4), ("gla_gain", 1), ("mix_post", 8), ("ffn_pre", 8),
                  ("ffn_post", 8), ("conv_b", 44), ("conv_w0", 44), ("conv_w1", 44), ("conv_w2", 44),
                  ("mix2", 8), ("mu", 14), ("w0", 8), ("a0", 8), ("k_k", 4), ("k_a", 4), ("r_k", 8),
                  ("lnx_w", 4), ("lnx_b", 4), ("ffn2", 8), ("ple", 8)):
    PARAMS[_name] = (_at, _n)
    _at += _n
N_PARAMS = _at

CONSTS = {}
_at = 0
for _name, _n in (("ident", P), ("ones", P), ("head_ones", P), ("le", P), ("gt", P), ("ge", P), ("lt", P),
                  ("flip", P), ("win", NA_COLS)):
    CONSTS[_name] = (_at, _n)
    _at += _n
N_CONSTS = _at
CONSTS2 = {}
_at = 0
for _name, _n in (("band", 3 * P), ("cos", NB * ROT), ("sin", NB * ROT), ("scan", GRID)):
    CONSTS2[_name] = (_at, _n)
    _at += _n
N_CONSTS2 = _at
LEVELS = 6


def shape_constants():
    c = np.zeros((P, N_CONSTS), np.float32)
    c2 = np.zeros((P, N_CONSTS2), np.float32)

    def put(name, a):
        table, to = (CONSTS, c) if name in CONSTS else (CONSTS2, c2)
        at, n = table[name]
        to[:, at:at + n] = a

    i = np.arange(P)
    p, f = i[:, None], i[None, :]
    same = p // CH == f // CH
    put("ident", p == f)
    put("ones", 1.0)
    put("head_ones", same)
    put("le", same & (p <= f))
    put("ge", same & (p >= f))
    put("lt", same & (p < f))
    put("gt", same & (p > f))
    put("flip", same & (p % CH == CH - 1 - f % CH))
    cq, ck = (i % NA_COLS)[:, None], np.arange(NA_COLS)[None, :]
    cs = np.clip(cq - WIN // 2, 0, NA_COLS - WIN)
    put("win", np.where((ck >= cs) & (ck < cs + WIN), 0.0, NEG))
    kk = np.arange(3 * P)[None, :] - P
    put("band", np.where(np.abs(p - kk) <= WINDOW, 0.0, NEG))
    inv = np.power(np.float32(500000.0), -np.arange(ROT, dtype=np.float32) * np.float32(2.0) / np.float32(16))
    ang = (np.arange(GRID, dtype=np.float32)[:, None] * inv[None, :].astype(np.float32)).astype(np.float32)
    ang = ang.reshape(NB, P, ROT).transpose(1, 0, 2).reshape(P, NB * ROT)
    put("cos", np.cos(ang))
    put("sin", np.sin(ang))
    put("scan", (np.arange(GRID) % CH != 0)[None, :])
    m = np.zeros((P, 2, LEVELS, P), np.float32)
    for k in range(LEVELS):
        block = (p >> (k + 1)) == (f >> (k + 1))
        m[:, 0, k] = block & ((p >> k) % 2 == 1) & ((f >> k) % 2 == 0)
        m[:, 1, k] = block & ((p >> k) % 2 == 0) & ((f >> k) % 2 == 1)
    return c, c2, m.reshape(P, -1)


def past(j, k):
    return not isinstance(j, int) or j >= k


class Phase:

    def __init__(self, n0, c0, count, tiles, before):
        self.n0, self.c0, self.count, self.tiles, self.before = n0, c0, count, tiles, before
        self.more = False

    def done(self, j):
        return self.c0 + self.tiles * (j + 1)

    def end(self):
        return self.done(self.count - 1)

    def done_before(self, j):
        if past(j, 1):
            return self.done(j - 1)
        return self.before.end() if self.before else None


class Ring:

    def __init__(self, ctx, nc, tag):
        def sem(name):
            return nc.alloc_semaphore(f"{tag}_{name}")

        def sb(name, dt):
            return ctx.enter_context(nc.sbuf_tensor(f"{tag}_{name}", [P, 2, KT * SLOT], dt))

        self.raw, self.hi, self.lo = sb("w_raw", F32), sb("w_hi", F32R), sb("w_lo", F32R)
        self.loaded = [sem("w_loaded0"), sem("w_loaded1")]
        self.hi_done = sem("w_hi_done")
        self.split = sem("w_split")
        self.tile_done = sem("tile_done")
        self.tile_free = sem("tile_free")
        self.phases = []

    def phase(self, count, tiles=2):
        before = self.phases[-1] if self.phases else None
        p = Phase(before.n0 + before.count if before else 0, before.end() if before else 0, count, tiles, before)
        if before:
            before.more = True
        self.phases.append(p)
        return p


def each_slot(eng, ph, body):
    def peeled(j):
        body(j, (ph.n0 + j) // 2, (ph.n0 + j) % 2)

    head = 2 + ph.n0 % 2
    pairs = (ph.count - head - 1) // 2
    if pairs < 2:
        for j in range(ph.count):
            peeled(j)
        return
    for j in range(head):
        peeled(j)
    with eng.Fori(0, pairs) as i:
        for r in range(2):
            body(head + 2 * i + r, (ph.n0 + head) // 2 + i, r)
    for j in range(head + 2 * pairs, ph.count):
        peeled(j)


def load_phase(sp, R, ph, src, size=KT * SLOT):
    def load(j, q, r):
        if past(ph.n0, 2) or past(j, 2 - ph.n0):
            sp.wait_ge(R.split, 2 * q + r - 1)
        sp.dma_start(R.raw[:, r, 0:size], src[bass.ds(j, 1), :, :].rearrange("o p n -> p (o n)")).then_inc(R.loaded[r], 16)

    each_slot(sp, ph, load)


def hi_slot(act, nc, R, q, r, free, size=KT * SLOT):
    act.wait_ge(R.loaded[r], 16 * q + 16)
    if free is not None:
        act.wait_ge(R.tile_done, free)
    nc.scalar.activation(R.hi[:, r, 0:size], R.raw[:, r, 0:size], ACT.Copy).then_inc(R.hi_done, 1)


def hi_next(act, nc, R, ph, j, q, r):
    if isinstance(j, int) and j == ph.count - 1 and not ph.more:
        return
    hi_slot(act, nc, R, q + r, 1 - r, ph.done_before(j))


def lo_slot(dve, nc, R, q, r, size=KT * SLOT):
    dve.wait_ge(R.hi_done, 2 * q + r + 1)
    nc.vector.tensor_tensor(R.lo[:, r, 0:size], R.raw[:, r, 0:size], R.hi[:, r, 0:size].bitcast(F32),
                            ALU.subtract).then_inc(R.split, 1)


def lo_next(dve, nc, R, ph, j, q, r):
    if isinstance(j, int) and j == ph.count - 1 and not ph.more:
        return
    lo_slot(dve, nc, R, q + r, 1 - r)


def three_pass(nc, out, w_hi, w_lo, u_hi, u_lo, start, stop):
    nc.tensor.matmul(out, w_hi, u_hi, start=start, stop=False)
    nc.tensor.matmul(out, w_lo, u_hi, start=False, stop=False)
    return nc.tensor.matmul(out, w_hi, u_lo, start=False, stop=stop)


def slots_in(R):
    return R.phases[-1].n0 + R.phases[-1].count


def hi_ahead(act, nc, R, ph, j, q, r):
    if isinstance(j, int) and ph.n0 + j + 2 >= slots_in(R):
        return
    hi_slot(act, nc, R, q + 1, r, ph.done(j))


def lo_ahead(dve, nc, R, ph, j, q, r):
    if isinstance(j, int) and ph.n0 + j + 2 >= slots_in(R):
        return
    lo_slot(dve, nc, R, q + 1, r)


def gemm_slot(pe, nc, R, ph, j, q, r, u_hi, u_lo, outs, rows=range(KT), cols=SLOT, ready=None):
    pe.wait_ge(R.split, 2 * q + r + 1)
    for m in range(ph.tiles):
        place = (r * ph.tiles + m) % len(outs)
        t = ph.tiles * j + m
        if past(j, (len(outs) + ph.tiles - 1) // ph.tiles) or (isinstance(t, int) and t >= len(outs)):
            pe.wait_ge(R.tile_free, ph.c0 + t - len(outs) + 1)
        elif m == 0 and isinstance(j, int) and j == 0 and ph.c0:
            pe.wait_ge(R.tile_free, ph.c0)
        for part, (out, tok) in enumerate(outs[place]):
            for k, row in enumerate(rows):
                if ready and part == 0 and isinstance(t, int) and t == 0:
                    pe.wait_ge(ready[0], ready[1] + k + 1)
                at = k * cols + m * P
                last = three_pass(nc, out, R.hi[:, r, at:at + P], R.lo[:, r, at:at + P],
                                  u_hi[:, row, tok], u_lo[:, row, tok], k == 0, k == len(rows) - 1)
        last.then_inc(R.tile_done, 1)


def norm_square(act, nc, x, sq, free, squared, tokens, loaded):
    for k in range(KT):
        if k % 2 == 0:
            act.wait_ge(loaded[k // 2], 16)
        if k >= 2:
            act.wait_ge(free, k - 1)
        nc.scalar.activation(sq[:, k % 2, 0:tokens], x[:, k, :], ACT.Square).then_inc(squared, 1)


def norm_sum(pe, nc, ones, sq, squared, summed, outs):
    for k in range(KT):
        pe.wait_ge(squared, k + 1)
        for out, tok in outs:
            last = nc.tensor.matmul(out, ones, sq[:, k % 2, tok], start=k == 0, stop=k == KT - 1)
        last.then_inc(summed, 1)


def add_squares(pool, nc, sq, total, squared, added, n=0):
    for k in range(KT):
        pool.wait_ge(squared, KT * n + k + 1)
        if k:
            pool.wait_ge(added, KT * n + k)
            nc.gpsimd.tensor_tensor(total, total, sq[:, k % 2, :], ALU.add).then_inc(added, 1)
        else:
            nc.gpsimd.tensor_copy(total, sq[:, k % 2, :]).then_inc(added, 1)


def next_squares(act, nc, h, sq, added, sq_added, squared):
    for k in range(KT):
        act.wait_ge(added, k + 1)
        act.wait_ge(sq_added, KT + k - 1)
        nc.scalar.activation(sq[:, k % 2, :], h[:, k, :], ACT.Square).then_inc(squared, 1)


def sum_over_features(pe, nc, C, bank, sq_sum, sq_added, summed, n):
    pe.wait_ge(sq_added, KT * n)
    for i in range(2):
        last = nc.tensor.matmul(bank[:, 4 + i, 0:HALF], C("ones"), sq_sum[:, i * HALF:i * HALF + HALF], start=True, stop=True)
    last.then_inc(summed, 1)


def mixer_block(nc, io, C, PV, h, rms):
    with ExitStack() as ctx:
        def sem(name):
            return nc.alloc_semaphore(f"m_{name}")

        def sb(name, shape, dt=F32):
            return ctx.enter_context(nc.sbuf_tensor(f"m_{name}", shape, dt))

        R = Ring(ctx, nc, "m")
        fm = R.phase(6)
        tm = R.phase(6, 5)
        zz = R.phase(1, 1)
        u_hi, u_lo = sb("u_hi", [P, KT, L], F32R), sb("u_lo", [P, KT, L], F32R)
        proj = sb("proj", [P, 13, L])
        vg = sb("vg", [P, 5, 1536])
        bank = ctx.enter_context(nc.psum_tensor("m_bank", [P, 8, 512], F32))
        eye = C("ident")

        def gain(name, k=0):
            at = PARAMS[name][0] + k
            return PV[:, at:at + 1]

        squared, summed, std_done, rs_done = sem("squared"), sem("summed"), sem("std_done"), sem("rs_done")
        normed, u_hi_done, u_done = sem("normed"), sem("u_hi_done"), sem("u_done")
        const_loaded = sem("const_loaded")
        h_loaded = [sem(f"h_loaded{k}") for k in range(4)]
        halves = [slice(0, HALF), slice(HALF, L)]

        with ExitStack() as inner:
            def sbi(name, shape, dt=F32):
                return inner.enter_context(nc.sbuf_tensor(f"m_{name}", shape, dt))

            bias = sbi("bias", [P, NA_H, RPB_R - 1, NA_COLS])
            s = sbi("s", [P, 2, L])
            pt = sbi("pt", [P, 2, 512])
            ptm = sbi("ptm", [META, 2, P])
            om = sbi("om", [META, 512])
            sm = sbi("sm", [META, 8, META])
            st = sbi("st", [P, 160])
            rs = s[:, 1, :]
            sq = bias[:, 0:3, :, :].rearrange("p a b c -> p (a b c)")[:, 0:2 * L].rearrange("p (a b) -> p a b", a=2)
            unit = s[:, 0, :]

            bias_loaded, flipped, masked = sem("bias_loaded"), sem("bias_flipped"), sem("bias_masked")
            s_done, s_read, s_meta, mx_done, p_done, r_done = (sem(x) for x in
                                                              ("s_done", "s_read", "s_meta", "mx_done", "p_done", "r_done"))
            t_done, pt_copied, ptm_copied, o_done, o_read = (sem(x) for x in
                                                             ("t_done", "pt_copied", "ptm_copied", "o_done", "o_read"))
            ms_done, ms, mp_done, mt_done, mt_copied, mo_done, mo_read = (
                sem(x) for x in ("ms_done", "ms", "mp_done", "mt_done", "mt_copied", "mo_done", "mo_read"))
            ss_done, na_std, na_rs, on_done, ot_done, mix_hi, mix_lo = (
                sem(x) for x in ("ss_done", "na_std", "na_rs", "on_done", "ot_done", "mix_hi", "mix_lo"))
            nm = st[:, 0:2]
            den = st[:, 2:34]
            rden = st[:, 34:66]
            ss = st[:, 66:71]
            nrs = st[:, 71:76]
            mmx = st[0:META, 76:84]
            msum = st[0:META, 84:92]
            NI = NB * NA_H

            def gbuf(t):
                return proj[:, 0:4, META + P * t:META + P * t + P]

            def tokens_of(t):
                return slice(META + P * t, META + P * t + P) if t < 4 else slice(0, META)

            def mix_part(act, t):
                n = P if t < 4 else META
                act.wait_ge(ot_done, t + 1)
                for f in range(4):
                    nc.scalar.activation(u_hi[:, f, tokens_of(t)], bank[:, t % 2, f * P:f * P + n], ACT.Copy,
                                         scale=gain("na_gain", f)).then_inc(mix_hi, 1)

            block = inner.enter_context(nc.Block())

            @block.sync
            def _(sp):
                for k in range(4):
                    sp.dma_start(h[:, 2 * k:2 * k + 2, :], io["h"][:, 2 * k:2 * k + 2, :]).then_inc(h_loaded[k], 16)
                w = io["w_in"]
                load_phase(sp, R, fm, w[0:6])
                load_phase(sp, R, tm, w[6:12])
                load_phase(sp, R, zz, w[12:13])

            @block.gpsimd
            def _(pool):
                pool.wait_ge(u_done, KT)
                rp = io["rpb"]
                for a in range(2):
                    for hh in range(NA_H):
                        src = bass.AP(tensor=rp.tensor, offset=(hh * RPB_R + 1 - a) * PAD_C,
                                      ap=[[1, NA_COLS], [PAD_C, RPB_R - 1], [1, NA_COLS]])
                        pool.dma_start(bias[64 * a:64 * a + 64, hh, :, :], src).then_inc(bias_loaded, 16)

            @block.scalar
            def _(act):
                act.dma_start(C.all[:], io["consts"]).then_inc(const_loaded, 16)
                act.dma_start(PV[:], io["params"]).then_inc(const_loaded, 16)
                norm_square(act, nc, h, sq, summed, squared, L, h_loaded)
                hi_slot(act, nc, R, 0, 0, None)
                act.wait_ge(summed, KT)
                nc.scalar.activation(unit, bank[:, 4:6, 0:HALF], ACT.Sqrt, scale=1.0 / D, bias=EPS).then_inc(std_done, 1)
                for k in range(KT):
                    act.wait_ge(normed, k + 1)
                    nc.scalar.activation(u_hi[:, k, :], sq[:, k % 2, :], ACT.Copy).then_inc(u_hi_done, 1)

                def fm_slot(j, q, r):
                    hi_next(act, nc, R, fm, j, q, r)
                    for m in range(2):
                        act.wait_ge(R.tile_done, fm.c0 + 2 * j + m + 1)
                        nc.scalar.activation(proj[:, bass.ds(2 * j + m, 1), :].rearrange("p o (a b) -> p (o a) b", a=2),
                                             bank[:, 2 * m:2 * m + 2, 0:HALF], ACT.Copy).then_inc(R.tile_free, 1)

                each_slot(act, fm, fm_slot)

                def tm_slot(j, q, r):
                    hi_next(act, nc, R, tm, j, q, r)
                    for t in range(5):
                        n = P if t < 4 else META
                        act.wait_ge(R.tile_done, tm.c0 + 5 * j + t + 1)
                        nc.scalar.activation(vg[0:n, t, bass.ds(SLOT * j, SLOT)], bank[0:n, 3 + t, 0:SLOT],
                                             ACT.Copy).then_inc(R.tile_free, 1)

                each_slot(act, tm, tm_slot)
                act.wait_ge(R.tile_done, zz.end())
                nc.scalar.activation(proj[:, 12, :].rearrange("p (a b) -> p a b", a=2), bank[:, 0:2, 0:HALF],
                                     ACT.Copy).then_inc(R.tile_free, 1)

                def read_o(i):
                    t, hh = divmod(i, NA_H)
                    act.wait_ge(o_done, i + 1)
                    act.wait_ge(r_done, i + 1)
                    b = 2 * (i % 2) + 1
                    dst = proj[:, hh // 2, META + P * t + 64 * (hh % 2):META + P * t + 64 * (hh % 2) + 64]
                    nc.scalar.activation(dst, bank[:, b, P + 64 * (hh % 2):P + 64 * (hh % 2) + 64], ACT.Copy,
                                         scale=rden[:, i:i + 1]).then_inc(o_read, 1)

                def copy_ptm(i):
                    act.wait_ge(t_done, i + 1)
                    if i >= 2:
                        act.wait_ge(o_done, i - 1)
                    nc.scalar.activation(ptm[:, i % 2, :], bank[0:META, 2 * (i % 2) + 1, 0:P], ACT.Copy).then_inc(ptm_copied, 1)

                for i in range(NI):
                    act.wait_ge(s_done, i + 1)
                    if i >= 2:
                        act.wait_ge(t_done, i - 1)
                    nc.scalar.activation(s[:, i % 2, GRID:L], bank[:, 5 + 2 * (i % 2), 0:META], ACT.Copy,
                                         scale=0.125).then_inc(s_meta, 1)
                    act.wait_ge(mx_done, i + 1)
                    nc.scalar.activation(s[:, i % 2, :], s[:, i % 2, :], ACT.Exp, bias=nm[:, i % 2:i % 2 + 1],
                                         accum_out=den[:, i:i + 1]).then_inc(p_done, 1)
                    if i >= 1:
                        copy_ptm(i - 1)
                    if i >= 2:
                        read_o(i - 2)
                copy_ptm(NI - 1)
                read_o(NI - 2)
                read_o(NI - 1)
                act.wait_ge(ms, 3)
                nc.scalar.activation(sm[:], sm[:], ACT.Exp).then_inc(mp_done, 1)
                act.wait_ge(mt_done, 1)
                nc.scalar.activation(ptm[:, 0, :], bank[0:META, 5, 0:P], ACT.Copy).then_inc(mt_copied, 1)
                act.wait_ge(mo_done, 1)
                nc.scalar.activation(om[:], bank[0:META, 6, :], ACT.Copy).then_inc(mo_read, 1)
                act.wait_ge(o_read, NI)
                act.wait_ge(mo_read, 1)
                act.wait_ge(t_done, NI)
                for t in range(NB):
                    if t:
                        act.wait_ge(ss_done, t)
                    nc.scalar.activation(s[:, 0, 0:512].rearrange("p (a b) -> p a b", a=4), gbuf(t), ACT.Square,
                                         accum_out=ss[:, t:t + 1]).then_inc(ss_done, 1)
                act.wait_ge(ss_done, NB)
                nc.scalar.activation(s[0:META, 0, 0:512], om[:], ACT.Square, accum_out=ss[0:META, 4:5]).then_inc(ss_done, 1)
                act.wait_ge(ss_done, NB + 1)
                nc.scalar.activation(nrs[:, 0:4], ss[:, 0:4], ACT.Sqrt, scale=1.0 / 512, bias=EPS).then_inc(na_std, 1)
                nc.scalar.activation(nrs[0:META, 4:5], ss[0:META, 4:5], ACT.Sqrt, scale=1.0 / 512, bias=EPS).then_inc(na_std, 1)
                act.wait_ge(na_rs, 2)
                for t in range(5):
                    n = P if t < 4 else META
                    src = gbuf(t) if t < 4 else om[:].rearrange("p (a b) -> p a b", a=4)
                    if t >= 2:
                        act.wait_ge(ot_done, t - 1)
                    nc.scalar.activation(s[0:n, t % 2, 0:512].rearrange("p (a b) -> p a b", a=4), src, ACT.Copy,
                                         scale=nrs[0:n, t:t + 1]).then_inc(on_done, 1)
                    if t >= 1:
                        mix_part(act, t - 1)
                mix_part(act, 4)

            @block.vector
            def _(dve):
                dve.wait_ge(const_loaded, 32)
                lo_slot(dve, nc, R, 0, 0)
                dve.wait_ge(std_done, 1)
                nc.vector.reciprocal(rs, unit).then_inc(rs_done, 1)
                dve.wait_ge(rs_done, 1)
                for k in range(KT):
                    if k >= 2:
                        dve.wait_ge(u_done, k - 1)
                    nc.vector.scalar_tensor_tensor(sq[:, k % 2, :], h[:, k, :], gain("mix_pre", k), rs,
                                                   ALU.mult, ALU.mult).then_inc(normed, 1)
                    dve.wait_ge(u_hi_done, k + 1)
                    nc.vector.tensor_tensor(u_lo[:, k, :], sq[:, k % 2, :], u_hi[:, k, :].bitcast(F32),
                                            ALU.subtract).then_inc(u_done, 1)
                for ph in (fm, tm, zz):
                    each_slot(dve, ph, lambda j, q, r, ph=ph: lo_next(dve, nc, R, ph, j, q, r))

                def copy_pt(i):
                    dve.wait_ge(p_done, i + 1)
                    nc.vector.reciprocal(rden[:, i:i + 1], den[:, i:i + 1]).then_inc(r_done, 1)
                    dve.wait_ge(t_done, i + 1)
                    if i >= 2:
                        dve.wait_ge(o_done, i - 1)
                    nc.vector.tensor_copy(pt[:, i % 2, :], bank[:, 2 * (i % 2), :]).then_inc(pt_copied, 1)

                for i in range(2 * NA_H):
                    dve.wait_ge(flipped, i + 1)
                    rows = bias[:, i // 2, 7 * (i % 2):7 * (i % 2) + 7, :]
                    nc.vector.tensor_tensor(rows, bank[:, 4 + i % 4, 0:7 * NA_COLS].rearrange("p (a b) -> p a b", a=7),
                                            C("win").unsqueeze(1).broadcast_to([P, 7, NA_COLS]), ALU.add).then_inc(masked, 1)
                dve.wait_ge(masked, 2 * NA_H)
                for i in range(NI):
                    t, hh = divmod(i, NA_H)
                    dve.wait_ge(s_done, i + 1)
                    if i >= 2:
                        dve.wait_ge(t_done, i - 1)
                    rows = bias[:, hh, 6 - 2 * t:14 - 2 * t, :].rearrange("p a b -> p (a b)")
                    nc.vector.scalar_tensor_tensor(s[:, i % 2, 0:GRID], bank[:, 4 + 2 * (i % 2), :], 0.125, rows,
                                                   ALU.mult, ALU.add).then_inc(s_read, 1)
                    dve.wait_ge(s_read, i + 1)
                    dve.wait_ge(s_meta, i + 1)
                    nc.vector.tensor_reduce(nm[:, i % 2:i % 2 + 1], s[:, i % 2, :], X, ALU.max, negate=True).then_inc(mx_done, 1)
                    if i >= 1:
                        copy_pt(i - 1)
                copy_pt(NI - 1)
                dve.wait_ge(ms_done, 1)
                nc.vector.tensor_scalar(sm[:, 0:8:2, :], bank[0:META, 4, 0:64].rearrange("p (a b) -> p a b", a=4), 0.125, None,
                                        ALU.mult)
                nc.vector.tensor_scalar(sm[:, 1:8:2, :], bank[0:META, 7, 0:64].rearrange("p (a b) -> p a b", a=4), 0.125, None,
                                        ALU.mult).then_inc(ms, 1)
                dve.wait_ge(ms, 1)
                nc.vector.tensor_reduce(mmx, sm[:], X, ALU.max).then_inc(ms, 1)
                dve.wait_ge(ms, 2)
                nc.vector.tensor_tensor(sm[:], sm[:], mmx.unsqueeze(2).broadcast_to([META, 8, META]), ALU.subtract).then_inc(ms, 1)
                dve.wait_ge(mp_done, 1)
                nc.vector.tensor_reduce(msum, sm[:], X, ALU.add).then_inc(ms, 1)
                dve.wait_ge(ms, 4)
                nc.vector.reciprocal(mmx, msum).then_inc(ms, 1)
                dve.wait_ge(ms, 5)
                nc.vector.tensor_tensor(sm[:], sm[:], mmx.unsqueeze(2).broadcast_to([META, 8, META]), ALU.mult).then_inc(ms, 1)
                dve.wait_ge(na_std, 2)
                nc.vector.reciprocal(nrs[:, 0:4], nrs[:, 0:4]).then_inc(na_rs, 1)
                nc.vector.reciprocal(nrs[0:META, 4:5], nrs[0:META, 4:5]).then_inc(na_rs, 1)
                for t in range(5):
                    n = P if t < 4 else META
                    dve.wait_ge(mix_hi, 4 * (t + 1))
                    for f in range(4):
                        last = nc.vector.scalar_tensor_tensor(
                            u_lo[:, f, tokens_of(t)], bank[:, t % 2, f * P:f * P + n], gain("na_gain", f),
                            u_hi[:, f, tokens_of(t)].bitcast(F32), ALU.mult, ALU.subtract)
                    last.then_inc(mix_lo, 1)

            @block.tensor
            def _(pe):
                pe.wait_ge(const_loaded, 32)
                norm_sum(pe, nc, C("ones"), sq, squared, summed,
                         [(bank[:, 4 + i, 0:HALF], halves[i]) for i in range(2)])
                pair = [[(bank[:, 2 * m + i, 0:HALF], halves[i]) for i in range(2)] for m in range(2)]
                each_slot(pe, fm, lambda j, q, r: gemm_slot(pe, nc, R, fm, j, q, r, u_hi, u_lo, pair, ready=(u_done, 0)))

                def tm_slot(j, q, r):
                    pe.wait_ge(R.split, 2 * q + r + 1)
                    for t in range(5):
                        if past(j, 1):
                            pe.wait_ge(R.tile_free, tm.c0 + 5 * (j - 1) + t + 1)
                        elif t == 0:
                            pe.wait_ge(R.tile_free, tm.c0)
                        n, tok = (P, slice(META + P * t, META + P * t + P)) if t < 4 else (META, slice(0, META))
                        for k in range(KT):
                            w = slice(k * SLOT, k * SLOT + SLOT)
                            out = bank[0:n, 3 + t, 0:SLOT]
                            nc.tensor.matmul(out, u_hi[:, k, tok], R.hi[:, r, w], start=k == 0, stop=False)
                            nc.tensor.matmul(out, u_lo[:, k, tok], R.hi[:, r, w], start=False, stop=False)
                            last = nc.tensor.matmul(out, u_hi[:, k, tok], R.lo[:, r, w], start=False, stop=k == KT - 1)
                        last.then_inc(R.tile_done, 1)

                each_slot(pe, tm, tm_slot)
                each_slot(pe, zz, lambda j, q, r: gemm_slot(pe, nc, R, zz, j, q, r, u_hi, u_lo, pair))
                pe.wait_ge(R.tile_free, zz.end())
                pe.wait_ge(bias_loaded, 16 * 2 * NA_H)
                for i in range(2 * NA_H):
                    if i >= 4:
                        pe.wait_ge(masked, i - 3)
                    rows = bias[:, i // 2, 7 * (i % 2):7 * (i % 2) + 7, :].rearrange("p a b -> p (a b)")
                    nc.tensor.matmul(bank[:, 4 + i % 4, 0:7 * NA_COLS], C("flip"), rows, start=True, stop=True).then_inc(flipped, 1)
                pe.wait_ge(masked, 2 * NA_H)

                def scores(i):
                    t, hh = divmod(i, NA_H)
                    if i >= 2:
                        pe.wait_ge(s_read, i - 1)
                        pe.wait_ge(s_meta, i - 1)
                    hp = slice(64 * (hh % 2), 64 * (hh % 2) + 64)
                    q = proj[hp, hh // 2, META + P * t:META + P * t + P]
                    nc.tensor.matmul(bank[:, 4 + 2 * (i % 2), :], q, proj[hp, 4 + hh // 2, META:L], start=True, stop=True)
                    nc.tensor.matmul(bank[:, 5 + 2 * (i % 2), 0:META], q, proj[hp, 4 + hh // 2, 0:META],
                                     start=True, stop=True).then_inc(s_done, 1)

                def turn(i):
                    pe.wait_ge(p_done, i + 1)
                    if i >= 2:
                        pe.wait_ge(pt_copied, i - 1)
                        pe.wait_ge(o_read, i - 1)
                    b = 2 * (i % 2)
                    for k in range(4):
                        nc.tensor.transpose(bank[:, b, k * P:k * P + P], s[:, i % 2, k * P:k * P + P], eye)
                    nc.tensor.transpose(bank[0:META, b + 1, 0:P], s[:, i % 2, GRID:L], eye).then_inc(t_done, 1)

                def values(i):
                    hh = i % NA_H
                    pe.wait_ge(pt_copied, i + 1)
                    pe.wait_ge(ptm_copied, i + 1)
                    b = 2 * (i % 2) + 1
                    cols = slice(P * (hh // 2), P * (hh // 2) + P)
                    for k in range(4):
                        nc.tensor.matmul(bank[:, b, P:2 * P], pt[:, i % 2, k * P:k * P + P], vg[:, k, cols],
                                         start=k == 0, stop=False)
                    nc.tensor.matmul(bank[:, b, P:2 * P], ptm[:, i % 2, :], vg[0:META, 4, cols],
                                     start=False, stop=True).then_inc(o_done, 1)

                scores(0)
                for i in range(NI):
                    if i + 1 < NI:
                        scores(i + 1)
                    turn(i)
                    if i >= 1:
                        values(i - 1)
                values(NI - 1)
                pe.wait_ge(s_read, NI)
                pe.wait_ge(s_meta, NI)
                for hh in range(NA_H):
                    hp = slice(64 * (hh % 2), 64 * (hh % 2) + 64)
                    last = nc.tensor.matmul(bank[0:META, 4 + 3 * (hh % 2), hh // 2 * META:hh // 2 * META + META], proj[hp, hh // 2, 0:META],
                                            proj[hp, 4 + hh // 2, 0:META], start=True, stop=True)
                last.then_inc(ms_done, 1)
                pe.wait_ge(ms, 6)
                for hh in range(NA_H):
                    last = nc.tensor.transpose(bank[0:META, 5, hh * META:hh * META + META], sm[:, hh, :], eye[0:META, 0:META])
                last.then_inc(mt_done, 1)
                pe.wait_ge(mt_copied, 1)
                for hh in range(NA_H):
                    last = nc.tensor.matmul(bank[0:META, 6, hh * 64:hh * 64 + 64], ptm[:, 0, hh * META:hh * META + META],
                                            vg[0:META, 4, hh * 64:hh * 64 + 64], start=True, stop=True)
                last.then_inc(mo_done, 1)
                for t in range(5):
                    n = P if t < 4 else META
                    pe.wait_ge(on_done, t + 1)
                    if t >= 2:
                        pe.wait_ge(mix_lo, t - 1)
                    else:
                        pe.wait_ge(o_read, NI)
                    for f in range(4):
                        last = nc.tensor.transpose(bank[:, t % 2, f * P:f * P + n], s[0:n, t % 2, f * P:f * P + P], eye[0:n, 0:n])
                    last.then_inc(ot_done, 1)

        gla_part(nc, io, C, PV, h, rms, ctx, R, u_hi, u_lo, proj, vg, bank, gain, sem)


def gla_part(nc, io, C, PV, h, rms, outer, R, u_hi, u_lo, proj, vg, bank, gain, sem):
    wo = R.phase(4)
    with ExitStack() as ctx:
        def sb(name, shape, dt=F32):
            return ctx.enter_context(nc.sbuf_tensor(f"m_{name}", shape, dt))

        NCK = 1 + NCH
        up = sb("up", [33, 512])
        tmp = sb("tmp", [P, 2, 512])
        e_pos, e_neg, e_end = sb("e_pos", [P, 4, P]), sb("e_neg", [P, 4, P]), sb("e_end", [P, 2, 256])
        k_inv, k_end = sb("k_inv", [P, 4, P]), sb("k_end", [P, 2, 256])
        at = sb("at", [P, 2, 2, 2, P])
        state = sb("state", [P, 2, 2, NCK, GLA_DV])
        decay = sb("decay", [P, 2, 2, NCK])
        ssq = sb("ssq", [P, 5, 4])
        size = [P] * 4 + [META]
        tok = [slice(META + P * t, META + P * t + P) for t in range(4)] + [slice(0, META)]
        chunks = [[(0, 1 + 2 * t), (1, 2 + 2 * t)] for t in range(4)] + [[(0, 0)]]
        rows = lambda half, n: slice(64 * half, 64 * half + min(n, CH))
        LA = lambda t: vg[0:size[t], t, 0:512]
        V = lambda t, rr, h0, h1: vg[rr, t, 512 + h0 * P:512 + h1 * P]
        QD = lambda hp, i, tk: proj[hp, i, tk]

        up_loaded, ones_row = sem("up_loaded"), sem("ones_row")
        raw_done, ab, la_done = sem("raw_done"), sem("ab"), sem("la_done")
        sg_exp, sg, sg_done = sem("sg_exp"), sem("sg"), sem("sg_done")
        b_done, e_done, qk, a_done, a_masked = (sem(x) for x in ("b_done", "e_done", "qk", "a_done", "a_masked"))
        oi_done, oi_read, ds_done, ds_read, scan = (sem(x) for x in ("oi_done", "oi_read", "ds_done", "ds_read", "scan"))
        in_done, o_sum, osq, osq_sum = (sem(x) for x in ("in_done", "o_sum", "osq", "osq_sum"))
        g_std, g_rs, on2, ot2, mix_hi2, mix_lo2 = (sem(x) for x in ("g_std", "g_rs", "on2", "ot2", "mix_hi2", "mix_lo2"))
        squared, summed, std_done, rs_done = sem("p_squared"), sem("p_summed"), sem("p_std_done"), sem("p_rs_done")
        scaled, added = sem("p_scaled"), sem("p_added")
        sq = vg[:, 0:2, 0:L]
        std, rs, sq_sum = vg[:, 2, 0:L], vg[:, 3, 0:L], vg[:, 4, 0:L]
        sq_added = sem("sq_added")
        halves = [slice(0, HALF), slice(HALF, L)]
        pair = [[(bank[:, b + i, 0:HALF], halves[i]) for i in range(2)] for b in (0, 6)]
        QK = 8

        def sum_heads(dve, t):
            n = size[t]
            dve.wait_ge(osq, t + 1)
            nc.vector.tensor_reduce(ssq[0:n, t, :], tmp[0:n, t % 2, :].rearrange("p (a b) -> p a b", a=4), X, ALU.add).then_inc(osq_sum, 1)

        def mix_rest(dve, t):
            n = size[t]
            dve.wait_ge(mix_hi2, t + 1)
            nc.vector.scalar_tensor_tensor(u_lo[:, 4:8, tok[t]], bank[:, 4 + t % 2, :].rearrange("p (a b) -> p a b", a=4)[:, :, 0:n],
                                           gain("gla_gain"), u_hi[:, 4:8, tok[t]].bitcast(F32), ALU.mult, ALU.subtract).then_inc(mix_lo2, 1)

        block = ctx.enter_context(nc.Block())

        @block.sync
        def _(sp):
            sp.dma_start(up[:], io["gate_up"]).then_inc(up_loaded, 16)
            load_phase(sp, R, wo, io["w_o"])

        @block.gpsimd
        def _(pool):
            add_squares(pool, nc, sq, sq_sum, squared, sq_added)
            pool.wait_ge(summed, 1)
            add_squares(pool, nc, sq, sq_sum, squared, sq_added, 1)

        @block.tensor
        def _(pe):
            pe.wait_ge(up_loaded, 16)
            pe.wait_ge(ones_row, 1)
            for t in range(5):
                nc.tensor.matmul(bank[0:size[t], t, :], proj[0:33, 12, tok[t]], up[:], start=True, stop=True).then_inc(raw_done, 1)
            for t in range(5):
                n = size[t]
                pe.wait_ge(la_done, t + 1)
                if t == 0:
                    pe.wait_ge(la_done, 5)
                if t >= 1:
                    pe.wait_ge(e_done, 3 * t)
                    pe.wait_ge(qk, QK * t)
                for i in range(4):
                    tri = C("le") if i < 2 else C("ge")
                    nc.tensor.matmul(bank[:, 2, i * P:i * P + n], vg[0:n, t, i * P:i * P + P], tri[0:n, 0:n], start=True, stop=True)
                for d in range(2):
                    rest = C("gt") if d == 0 else C("lt")
                    nc.tensor.matmul(bank[0:n, 3, 256 * d:256 * d + 256], rest[0:n, 0:n], vg[0:n, t, 256 * d:256 * d + 256],
                                     start=True, stop=True)
                for fi in range(2):
                    last = nc.tensor.transpose(bank[0:n, 4, fi * P:fi * P + P], proj[:, 10 + fi, tok[t]], C("ident"))
                last.then_inc(b_done, 1)
                pe.wait_ge(qk, QK * (t + 1))
                if t >= 1:
                    pe.wait_ge(a_masked, 4 * t)
                for d in range(2):
                    for hh in range(4):
                        hp = slice(64 * (hh % 2), 64 * (hh % 2) + 64)
                        i = 2 * d + hh // 2
                        last = nc.tensor.matmul(bank[0:n, 5 + hh % 2, i * P:i * P + n], k_inv[hp, i, 0:n], QD(hp, i, tok[t]),
                                                start=True, stop=True)
                last.then_inc(a_done, 1)
                if t >= 1:
                    pe.wait_ge(ds_read, 2 * t)
                for half, c in chunks[t]:
                    rr = rows(half, n)
                    for d in range(2):
                        for hh in range(4):
                            hp = slice(64 * (hh % 2), 64 * (hh % 2) + 64)
                            i = 2 * d + hh // 2
                            last = nc.tensor.matmul(bank[hp, half, i * P:i * P + P], k_end[rr, d, hh * 64:hh * 64 + 64],
                                                    V(t, rr, hh, hh + 1), start=True, stop=True)
                last.then_inc(ds_done, 1)
                pe.wait_ge(a_masked, 4 * (t + 1))
                if t >= 1:
                    pe.wait_ge(oi_read, t)
                for hh in range(4):
                    for d in range(2):
                        last = nc.tensor.matmul(bank[0:n, 7, hh * P:hh * P + P], at[0:n, hh % 2, d, hh // 2, 0:n],
                                                V(t, slice(0, n), hh, hh + 1), start=d == 0, stop=d == 1)
                last.then_inc(oi_done, 1)
            pe.wait_ge(oi_read, 5)
            pe.wait_ge(scan, 28)
            for t in range(5):
                if t >= 2:
                    pe.wait_ge(o_sum, 2 * (t - 1))
                for half, c in chunks[t]:
                    rr = rows(half, size[t])
                    start = (META + CH * (c - 1)) if c else 0
                    tk = slice(start, start + (CH if c else META))
                    dirs = [(d, c - 1 if d == 0 else c + 1) for d in range(2)]
                    dirs = [(d, f) for d, f in dirs if 0 <= f < NCK]
                    for hh in range(4):
                        hp = slice(64 * (hh % 2), 64 * (hh % 2) + 64)
                        for d, front in dirs:
                            last = nc.tensor.matmul(bank[rr, 2 + 4 * (t % 2) + hh % 2, hh // 2 * P:hh // 2 * P + P], QD(hp, 2 * d + hh // 2, tk),
                                                    state[hp, d, hh // 2, front, :], start=(d, front) == dirs[0],
                                                    stop=(d, front) == dirs[-1])
                last.then_inc(in_done, 1)
            for t in range(5):
                n = size[t]
                pe.wait_ge(on2, t + 1)
                if t >= 2:
                    pe.wait_ge(mix_lo2, t - 1)
                for f in range(4):
                    last = nc.tensor.transpose(bank[:, 4 + t % 2, f * P:f * P + n], tmp[0:n, t % 2, f * P:f * P + P],
                                               C("ident")[0:n, 0:n])
                last.then_inc(ot2, 1)
            pe.wait_ge(mix_lo2, 5)
            each_slot(pe, wo, lambda j, q, r: gemm_slot(pe, nc, R, wo, j, q, r, u_hi, u_lo, pair))
            sum_over_features(pe, nc, C, bank, sq_sum, sq_added, summed, 1)
            pe.wait_ge(std_done, 1)
            sum_over_features(pe, nc, C, bank, sq_sum, sq_added, summed, 2)

        @block.scalar
        def _(act):
            for t in range(5):
                act.wait_ge(raw_done, t + 1)
                nc.scalar.activation(LA(t), bank[0:size[t], t, :], ACT.Abs).then_inc(ab, 1)
            for t in range(5):
                act.wait_ge(ab, t + 1)
                nc.scalar.activation(LA(t), LA(t), ACT.Exp, scale=-1.0).then_inc(ab, 1)
            for t in range(5):
                act.wait_ge(ab, 5 + t + 1)
                nc.scalar.activation(LA(t), LA(t), ACT.Ln, bias=1.0).then_inc(ab, 1)
            hi_slot(act, nc, R, 6, 1, None)
            for t in range(5):
                n = size[t]
                act.wait_ge(b_done, t + 1)
                if t >= 1:
                    act.wait_ge(qk, QK * t)
                src = bank[:, 2, :].rearrange("p (a b) -> p a b", a=4)[:, :, 0:n]
                nc.scalar.activation(e_pos[:, :, 0:n], src, ACT.Exp, scale=1.0 / 16).then_inc(e_done, 1)
                nc.scalar.activation(e_neg[:, :, 0:n], src, ACT.Exp, scale=-1.0 / 16).then_inc(e_done, 1)
                nc.scalar.activation(e_end[0:n, :, :].rearrange("p a b -> p (a b)"), bank[0:n, 3, :], ACT.Exp,
                                     scale=1.0 / 16).then_inc(e_done, 1)
                if t >= 2:
                    act.wait_ge(sg_done, t - 1)
                nc.scalar.activation(tmp[0:n, t % 2, :], vg[0:n, t, 1024:1536], ACT.Exp, scale=-1.0).then_inc(sg_exp, 1)
                act.wait_ge(oi_done, t + 1)
                act.wait_ge(ds_done, t + 1)
                nc.scalar.activation(V(t, slice(0, n), 0, 4), bank[0:n, 7, :], ACT.Copy).then_inc(oi_read, 1)
            for t in range(5):
                n = size[t]
                act.wait_ge(o_sum, 2 * (t + 1))
                if t >= 2:
                    act.wait_ge(osq_sum, t - 1)
                else:
                    act.wait_ge(sg_done, 5)
                nc.scalar.activation(tmp[0:n, t % 2, :], V(t, slice(0, n), 0, 4), ACT.Square).then_inc(osq, 1)
            act.wait_ge(osq_sum, 5)
            for nn, tt in ((P, slice(0, 4)), (META, slice(4, 5))):
                nc.scalar.activation(ssq[0:nn, tt, :], ssq[0:nn, tt, :], ACT.Sqrt, scale=1.0 / GLA_DV, bias=EPS).then_inc(g_std, 1)
            for t in range(5):
                n = size[t]
                act.wait_ge(ot2, t + 1)
                nc.scalar.activation(u_hi[:, 4:8, tok[t]], bank[:, 4 + t % 2, :].rearrange("p (a b) -> p a b", a=4)[:, :, 0:n],
                                     ACT.Copy, scale=gain("gla_gain")).then_inc(mix_hi2, 1)

            def wo_slot(j, q, r):
                hi_next(act, nc, R, wo, j, q, r)
                for m in range(2):
                    act.wait_ge(R.tile_done, wo.c0 + 2 * j + m + 1)
                    b = (0, 6)[m]
                    nc.scalar.activation(proj[:, 2 * j + m, :].rearrange("p (a b) -> p a b", a=2),
                                         bank[:, b:b + 2, 0:HALF], ACT.Copy).then_inc(R.tile_free, 1)
                for m in range(2):
                    t = 2 * j + m
                    act.wait_ge(R.tile_free, wo.c0 + t + 1)
                    if t >= 2:
                        act.wait_ge(sq_added, t - 1)
                    nc.scalar.activation(sq[:, t % 2, :], proj[:, t, :], ACT.Square).then_inc(squared, 1)

            each_slot(act, wo, wo_slot)
            act.wait_ge(summed, 1)
            nc.scalar.activation(std.rearrange("p (a b) -> p a b", a=2), bank[:, 4:6, 0:HALF], ACT.Sqrt,
                                 scale=1.0 / D, bias=EPS).then_inc(std_done, 1)
            next_squares(act, nc, h, sq, added, sq_added, squared)
            act.wait_ge(summed, 2)
            nc.scalar.activation(rms[:].rearrange("p (a b) -> p a b", a=2), bank[:, 4:6, 0:HALF], ACT.Sqrt,
                                 scale=1.0 / D, bias=EPS).then_inc(std_done, 1)

        @block.vector
        def _(dve):
            nc.vector.memset(proj[32:33, 12, :], 1.0).then_inc(ones_row, 1)
            for t in range(5):
                dve.wait_ge(ab, 10 + t + 1)
                nc.vector.scalar_tensor_tensor(LA(t), bank[0:size[t], t, :], 0.0, LA(t), ALU.min, ALU.subtract).then_inc(la_done, 1)

            def silu(t):
                n = size[t]
                dve.wait_ge(sg_exp, t + 1)
                nc.vector.tensor_scalar(tmp[0:n, t % 2, :], tmp[0:n, t % 2, :], 1.0, None, ALU.add).then_inc(sg, 1)
                dve.wait_ge(sg, 2 * t + 1)
                nc.vector.reciprocal(tmp[0:n, t % 2, :], tmp[0:n, t % 2, :]).then_inc(sg, 1)
                dve.wait_ge(sg, 2 * t + 2)
                g = vg[0:n, t, 1024:1536]
                nc.vector.tensor_tensor(g, g, tmp[0:n, t % 2, :], ALU.mult).then_inc(sg_done, 1)
            lo_slot(dve, nc, R, 6, 1)
            for t in range(5):
                n = size[t]
                dve.wait_ge(e_done, 3 * t + 3)
                if t >= 1:
                    dve.wait_ge(a_done, t)
                    dve.wait_ge(ds_done, t)
                for d in range(2):
                    i = slice(2 * d, 2 * d + 2)
                    nc.vector.scalar_tensor_tensor(QD(slice(0, P), i, tok[t]), proj[:, 8:10, tok[t]], 0.125,
                                                   e_pos[:, i, 0:n], ALU.mult, ALU.mult).then_inc(qk, 1)
                    nc.vector.tensor_tensor(k_inv[:, i, 0:n], proj[:, 10:12, tok[t]], e_neg[:, i, 0:n], ALU.mult).then_inc(qk, 1)
                    nc.vector.tensor_tensor(k_end[0:n, d, :], bank[0:n, 4, 0:256], e_end[0:n, d, :], ALU.mult).then_inc(qk, 1)
                    c0 = chunks[t][0][1]
                    cols = slice(min(n, CH) - 1, n, CH) if d == 0 else slice(0, n, CH)
                    nc.vector.tensor_copy(decay[:, d, :, c0:c0 + len(chunks[t])], e_pos[:, i, cols]).then_inc(qk, 1)
                dve.wait_ge(a_done, t + 1)
                if t >= 1:
                    dve.wait_ge(oi_done, t)
                for par in range(2):
                    for d in range(2):
                        mask = (C("le") if d == 0 else C("gt"))[0:n, 0:n].unsqueeze(1).broadcast_to([n, 2, n])
                        src = bank[0:n, 5 + par, :].rearrange("p (a b) -> p a b", a=4)[:, 2 * d:2 * d + 2, 0:n]
                        nc.vector.tensor_tensor(at[0:n, par, d, :, 0:n], src, mask, ALU.mult).then_inc(a_masked, 1)
                dve.wait_ge(ds_done, t + 1)
                for half, c in chunks[t]:
                    nc.vector.tensor_copy(state[:, :, :, c, :].rearrange("p a b v -> p (a b) v"),
                                          bank[:, half, :].rearrange("p (a v) -> p a v", a=4)).then_inc(ds_read, 1)
                silu(t)
            dve.wait_ge(ds_read, NCK)
            dve.wait_ge(qk, QK * 5)
            for step in range(1, NCH):
                for d in range(2):
                    c = step if d == 0 else NCH - step
                    front = c - 1 if d == 0 else c + 1
                    for fi in range(2):
                        if step > 1:
                            dve.wait_ge(scan, 4 * (step - 1))
                        nc.vector.scalar_tensor_tensor(state[:, d, fi, c, :], state[:, d, fi, front, :], decay[:, d, fi, c:c + 1],
                                                       state[:, d, fi, c, :], ALU.mult, ALU.add).then_inc(scan, 1)
            for t in range(5):
                n = size[t]
                dve.wait_ge(in_done, t + 1)
                dve.wait_ge(oi_read, t + 1)
                for par in range(2):
                    o = V(t, slice(0, n), 0, 4).rearrange("p (a b c) -> p a b c", a=2, b=2)[:, :, par, :]
                    src = bank[0:n, 2 + 4 * (t % 2) + par, 0:256].rearrange("p (a c) -> p a c", a=2)
                    nc.vector.tensor_tensor(o, src, o, ALU.add).then_inc(o_sum, 1)
                if t >= 1:
                    sum_heads(dve, t - 1)
            sum_heads(dve, 4)
            dve.wait_ge(g_std, 2)
            for nn, tt in ((P, slice(0, 4)), (META, slice(4, 5))):
                nc.vector.reciprocal(ssq[0:nn, tt, :], ssq[0:nn, tt, :]).then_inc(g_rs, 1)
            dve.wait_ge(g_rs, 2)
            for t in range(5):
                n = size[t]
                if t >= 2:
                    dve.wait_ge(ot2, t - 1)
                for hh in range(4):
                    last = nc.vector.scalar_tensor_tensor(tmp[0:n, t % 2, hh * P:hh * P + P], V(t, slice(0, n), hh, hh + 1),
                                                          ssq[0:n, t, hh:hh + 1], vg[0:n, t, 1024 + hh * P:1024 + hh * P + P],
                                                          ALU.mult, ALU.mult)
                last.then_inc(on2, 1)
                if t >= 1:
                    mix_rest(dve, t - 1)
            mix_rest(dve, 4)
            each_slot(dve, wo, lambda j, q, r: lo_next(dve, nc, R, wo, j, q, r))
            dve.wait_ge(std_done, 1)
            nc.vector.reciprocal(rs, std).then_inc(rs_done, 1)
            dve.wait_ge(rs_done, 1)
            for k in range(KT + 1):
                if k < KT:
                    nc.vector.scalar_tensor_tensor(proj[:, k, :], proj[:, k, :], gain("mix_post", k), rs, ALU.mult, ALU.mult).then_inc(scaled, 1)
                if k:
                    dve.wait_ge(scaled, k)
                    nc.vector.tensor_tensor(h[:, k - 1, :], h[:, k - 1, :], proj[:, k - 1, :], ALU.add).then_inc(added, 1)


def ffn_block(nc, io, C, PV, h, rms):
    with ExitStack() as ctx:
        def sem(name):
            return nc.alloc_semaphore(f"f_{name}")

        def sb(name, shape, dt=F32):
            return ctx.enter_context(nc.sbuf_tensor(f"f_{name}", shape, dt))

        def column(name, k=0):
            return PV[:, bass.ds(PARAMS[name][0] + k, 1)]

        R = Ring(ctx, nc, "f")
        groups = [(0, 9), (9, 8), (17, 5)]
        into, out = [], []
        for _, count in groups:
            into.append(R.phase(count))
            out.append(R.phase(4))
        places = [range(0, 8), [8, 0, 1, 2, 3, 4, 5, 6], [7, 0, 1, 2, 3, 4]]
        u_hi, u_lo = sb("u_hi", [P, KT, L], F32R), sb("u_lo", [P, KT, L], F32R)
        y_hi, y_lo = sb("y_hi", [P, 9, L], F32R), sb("y_lo", [P, 9, L], F32R)
        acc = sb("acc", [P, KT, L])
        a = sb("a", [P, 2, 2, L + 2])
        c = sb("c", [P, 2, 2, L])
        bank = ctx.enter_context(nc.psum_tensor("f_bank", [P, 8, 512], F32))
        sq, std, rs = c[:, 0], c[:, 1, 0], c[:, 1, 1]
        tmp = acc
        sq_sum = a[:, 0, 0, 0:L]
        sq_added = sem("sq_added")
        halves = [slice(0, HALF), slice(HALF, L)]
        outs = [[(bank[:, 2 * t + i, 0:HALF], halves[i]) for i in range(2)] for t in range(4)]
        rs_done, normed, u_hi_done, u_done = (sem(x) for x in ("rs_done", "normed", "u_hi_done", "u_done"))
        edges, taken, convd, gelu_done, y_made, y_hi_done, y_done = (
            sem(x) for x in ("edges", "taken", "convd", "gelu_done", "y_made", "y_hi_done", "y_done"))
        psquared, psummed, pstd, prs, scaled, added = (
            sem(x) for x in ("psquared", "psummed", "pstd", "prs", "scaled", "added"))

        block = ctx.enter_context(nc.Block())

        @block.sync
        def _(sp):
            for g, (t0, count) in enumerate(groups):
                load_phase(sp, R, into[g], io["w_ffn_in"][t0:t0 + count])
                load_phase(sp, R, out[g], io["w_ffn_out"][4 * g:4 * g + 4])

        @block.gpsimd
        def _(pool):
            add_squares(pool, nc, sq, sq_sum, psquared, sq_added)
            pool.wait_ge(psummed, 1)
            add_squares(pool, nc, sq, sq_sum, psquared, sq_added, 1)

        @block.tensor
        def _(pe):
            for g, (t0, count) in enumerate(groups):
                each_slot(pe, into[g], lambda j, q, r, ph=into[g], ready=(u_done, 0) if g == 0 else None:
                          gemm_slot(pe, nc, R, ph, j, q, r, u_hi, u_lo, outs, ready=ready))
                each_slot(pe, out[g], lambda j, q, r, ph=out[g], rows=places[g], ready=(y_done, 8 * g):
                          gemm_slot(pe, nc, R, ph, j, q, r, y_hi, y_lo, outs, rows, ready=ready))
            pe.wait_ge(R.tile_free, out[2].end())
            sum_over_features(pe, nc, C, bank, sq_sum, sq_added, psummed, 1)
            pe.wait_ge(pstd, 1)
            sum_over_features(pe, nc, C, bank, sq_sum, sq_added, psummed, 2)

        @block.scalar
        def _(act):
            for k in range(KT):
                if k == 4:
                    hi_slot(act, nc, R, 0, 0, None)
                act.wait_ge(normed, k + 1)
                nc.scalar.activation(u_hi[:, k, :], tmp[:, k, :], ACT.Copy).then_inc(u_hi_done, 1)
            hi_slot(act, nc, R, 0, 1, None)

            def hidden(ph, t0, j, q, r):
                t = t0 + j
                for m in range(2):
                    act.wait_ge(R.tile_done, ph.c0 + 2 * j + m + 1)
                    if past(t, 2):
                        act.wait_ge(y_made, t - 1)
                    src = bank[:, 2 * (2 * r + m):2 * (2 * r + m) + 2, 0:HALF]
                    nc.scalar.activation(a[:, r, m, 1:L + 1].rearrange("p (a b) -> p a b", a=2), src, ACT.Copy).then_inc(taken, 1)
                    if past(t, 2):
                        act.wait_ge(y_done, t - 1)
                    nc.scalar.activation(c[:, r, m, :].rearrange("p (a b) -> p a b", a=2), src, ACT.Identity,
                                         scale=column("conv_w1", FT * m + t), bias=column("conv_b", FT * m + t)).then_inc(R.tile_free, 1)
                hi_ahead(act, nc, R, ph, j, q, r)
                act.wait_ge(convd, 4 * t + 4)
                nc.scalar.activation(c[:, r, 1, :], c[:, r, 1, :], ACT.Gelu_apprx_tanh).then_inc(gelu_done, 1)
                act.wait_ge(y_made, t + 1)
                place = j
                if isinstance(t, int) and t == 16:
                    place = 7
                nc.scalar.activation(y_hi[:, bass.ds(place, 1), :].rearrange("p o n -> p (o n)"), c[:, r, 0, :], ACT.Copy).then_inc(y_hi_done, 1)

            def first_sum(j, q, r):
                for m in range(2):
                    act.wait_ge(R.tile_done, out[0].c0 + 2 * j + m + 1)
                    nc.scalar.activation(acc[:, bass.ds(2 * j + m, 1), :].rearrange("p o (a b) -> p (o a) b", a=2),
                                         bank[:, 2 * (2 * r + m):2 * (2 * r + m) + 2, 0:HALF],
                                         ACT.Copy).then_inc(R.tile_free, 1)
                hi_ahead(act, nc, R, out[0], j, q, r)

            for g, (t0, count) in enumerate(groups):
                each_slot(act, into[g], lambda j, q, r, g=g, t0=t0: hidden(into[g], t0, j, q, r))
                if g == 0:
                    each_slot(act, out[0], first_sum)
                elif g == 1:
                    each_slot(act, out[1], lambda j, q, r: hi_ahead(act, nc, R, out[1], j, q, r))
            for t in range(KT):
                act.wait_ge(R.tile_free, out[2].c0 + t + 1)
                if t >= 2:
                    act.wait_ge(sq_added, t - 1)
                nc.scalar.activation(sq[:, t % 2, :], acc[:, t, :], ACT.Square).then_inc(psquared, 1)
                if t % 2:
                    j = t // 2
                    hi_ahead(act, nc, R, out[2], j, (out[2].n0 + j) // 2, (out[2].n0 + j) % 2)
            act.wait_ge(psummed, 1)
            nc.scalar.activation(std.rearrange("p (a b) -> p a b", a=2), bank[:, 4:6, 0:HALF], ACT.Sqrt,
                                 scale=1.0 / D, bias=EPS).then_inc(pstd, 1)
            next_squares(act, nc, h, sq, added, sq_added, psquared)
            act.wait_ge(psummed, 2)
            nc.scalar.activation(rms[:].rearrange("p (a b) -> p a b", a=2), bank[:, 4:6, 0:HALF], ACT.Sqrt,
                                 scale=1.0 / D, bias=EPS).then_inc(pstd, 1)

        @block.vector
        def _(dve):
            nc.vector.memset(a[:, :, :, 0:1], 0.0).then_inc(edges, 1)
            nc.vector.memset(a[:, :, :, L + 1:L + 2], 0.0).then_inc(edges, 1)
            nc.vector.reciprocal(rs, rms[:]).then_inc(rs_done, 1)
            dve.wait_ge(rs_done, 1)
            for k in range(KT + 1):
                if k < KT:
                    nc.vector.scalar_tensor_tensor(tmp[:, k, :], h[:, k, :], column("ffn_pre", k), rs, ALU.mult, ALU.mult).then_inc(normed, 1)
                if k:
                    dve.wait_ge(u_hi_done, k)
                    nc.vector.tensor_tensor(u_lo[:, k - 1, :], tmp[:, k - 1, :], u_hi[:, k - 1, :].bitcast(F32), ALU.subtract).then_inc(u_done, 1)
                if k == 4:
                    lo_slot(dve, nc, R, 0, 0)
            lo_slot(dve, nc, R, 0, 1)
            dve.wait_ge(edges, 2)

            def hidden(ph, t0, j, q, r):
                t = t0 + j
                for m in range(2):
                    dve.wait_ge(taken, 2 * t + m + 1)
                    dve.wait_ge(R.tile_free, ph.c0 + 2 * j + m + 1)
                    nc.vector.scalar_tensor_tensor(c[:, r, m, :], a[:, r, m, 0:L], column("conv_w0", FT * m + t), c[:, r, m, :],
                                                   ALU.mult, ALU.add).then_inc(convd, 1)
                    dve.wait_ge(convd, 4 * t + 2 * m + 1)
                    nc.vector.scalar_tensor_tensor(c[:, r, m, :], a[:, r, m, 2:L + 2], column("conv_w2", FT * m + t), c[:, r, m, :],
                                                   ALU.mult, ALU.add).then_inc(convd, 1)
                lo_ahead(dve, nc, R, ph, j, q, r)
                dve.wait_ge(gelu_done, t + 1)
                nc.vector.tensor_tensor(c[:, r, 0, :], c[:, r, 0, :], c[:, r, 1, :], ALU.mult).then_inc(y_made, 1)
                dve.wait_ge(y_hi_done, t + 1)
                place = 7 if isinstance(t, int) and t == 16 else j
                at = (slice(None), bass.ds(place, 1), slice(None))
                nc.vector.tensor_tensor(y_lo[at].rearrange("p o n -> p (o n)"), c[:, r, 0, :],
                                        y_hi[at].bitcast(F32).rearrange("p o n -> p (o n)"), ALU.subtract).then_inc(y_done, 1)

            def more_sum(g, j, q, r):
                for m in range(2):
                    dve.wait_ge(R.tile_done, out[g].c0 + 2 * j + m + 1)
                    if past(j, 0) and m == 0 and isinstance(j, int) and j == 0:
                        dve.wait_ge(R.tile_free, out[g - 1].end())
                    at = acc[:, bass.ds(2 * j + m, 1), :].rearrange("p o (a b) -> p (o a) b", a=2)
                    b = 2 * (2 * r + m)
                    nc.vector.tensor_tensor(at, bank[:, b:b + 2, 0:HALF], at, ALU.add).then_inc(R.tile_free, 1)
                lo_ahead(dve, nc, R, out[g], j, q, r)

            for g, (t0, count) in enumerate(groups):
                each_slot(dve, into[g], lambda j, q, r, g=g, t0=t0: hidden(into[g], t0, j, q, r))
                if g == 0:
                    each_slot(dve, out[0], lambda j, q, r: lo_ahead(dve, nc, R, out[0], j, q, r))
                else:
                    each_slot(dve, out[g], lambda j, q, r, g=g: more_sum(g, j, q, r))
            dve.wait_ge(pstd, 1)
            nc.vector.reciprocal(rs, std).then_inc(prs, 1)
            dve.wait_ge(prs, 1)
            for k in range(KT + 1):
                if k < KT:
                    nc.vector.scalar_tensor_tensor(acc[:, k, :], acc[:, k, :], column("ffn_post", k), rs, ALU.mult, ALU.mult).then_inc(scaled, 1)
                if k:
                    dve.wait_ge(scaled, k)
                    nc.vector.tensor_tensor(h[:, k - 1, :], h[:, k - 1, :], acc[:, k - 1, :], ALU.add).then_inc(added, 1)


def attention_block(nc, io, C, PV, h, zr, attn_t, rms):
    with ExitStack() as ctx:
        def sem(name):
            return nc.alloc_semaphore(f"a_{name}")

        def sb(name, shape, dt=F32):
            return ctx.enter_context(nc.sbuf_tensor(f"a_{name}", shape, dt))

        def gain(name, k=0):
            at = PARAMS[name][0] + k
            return PV[:, at:at + 1]

        R = Ring(ctx, nc, "a")
        qkv = R.phase(3, 4)
        mixed = R.phase(7)
        x = h[:, :, META:L]
        u_hi, u_lo = sb("u_hi", [P, KT, GRID], F32R), sb("u_lo", [P, KT, GRID], F32R)
        tmp = sb("tmp", [P, KT, GRID])
        c2 = sb("consts2", [P, N_CONSTS2])
        tok = sb("qkv", [P, NB, 768])
        heads = sb("heads", [P, 10, HD])
        sinks = sb("sinks", [P, 8])
        q_t, k_t = sb("q_t", [P, 4, GRID]), sb("k_t", [P, GRID])
        s = sb("s", [P, 2, 3 * P + 1])
        pt = sb("pt", [P, 2, 3 * P])
        rope = sb("rope", [P, 4, 10, ROT])
        shift = sb("shift", [P, 2, GRID + 2])
        mu = sb("mu", [P, 2, 14])
        st = sb("st", [P, 160])
        nm, den, rden = st[:, 0:2], st[:, 2:34], st[:, 34:66]
        hs = st[:, 66:106].rearrange("p (a b) -> p a b", a=NB)
        bank = ctx.enter_context(nc.psum_tensor("a_bank", [P, 8, 512], F32))
        rs = rms[:, META:L]

        def const2(name):
            at, n = CONSTS2[name]
            return c2[:, at:at + n]

        rs_done, normed, u_hi_done, u_done = (sem(x_) for x_ in ("rs_done", "normed", "u_hi_done", "u_done"))
        small, mu_done, edges, taken, pairs_sum, shifted = (
            sem(x_) for x_ in ("small", "mu_done", "edges", "taken", "pairs_sum", "shifted"))
        hsq, hsum, hstd, hrs, hn, roped, tq, tq_read = (
            sem(x_) for x_ in ("hsq", "hsum", "hstd", "hrs", "hn", "roped", "tq", "tq_read"))
        s_done, s_read, s_sink, mx_done, p_done, r_done, t_done, pt_copied, o_done, o_read, ta, ta_read = (
            sem(x_) for x_ in ("s_done", "s_read", "s_sink", "mx_done", "p_done", "r_done", "t_done", "pt_copied",
                               "o_done", "o_read", "ta", "ta_read"))
        NI = 8 * NB
        cos = lambda t: const2("cos")[:, t * ROT:t * ROT + ROT].unsqueeze(1).broadcast_to([P, 10, ROT])
        sin = lambda t: const2("sin")[:, t * ROT:t * ROT + ROT].unsqueeze(1).broadcast_to([P, 10, ROT])
        qk = lambda t: tok[:, t, 0:640].rearrange("p (a b) -> p a b", a=10)
        RN = 6

        def keys(n):
            ks = [b for b in (n - 1, n, n + 1) if 0 <= b < NB]
            return ks, 3 * P - P * len(ks)

        block = ctx.enter_context(nc.Block())

        @block.sync
        def _(sp):
            g = io["qk_gain"]
            sp.dma_start(heads[:, 0:8, :], bass.AP(tensor=g.tensor, offset=0, ap=[[0, P], [0, 8], [1, HD]])).then_inc(small, 16)
            sp.dma_start(heads[:, 8:10, :], bass.AP(tensor=g.tensor, offset=HD, ap=[[0, P], [0, 2], [1, HD]])).then_inc(small, 16)
            sp.dma_start(sinks[:], bass.AP(tensor=io["sink"].tensor, offset=0, ap=[[0, P], [1, 8]])).then_inc(small, 16)
            sp.dma_start(c2[:], io["consts2"]).then_inc(small, 16)
            load_phase(sp, R, qkv, io["w_in2"][0:3])
            load_phase(sp, R, mixed, io["w_in2"][3:10])

        @block.tensor
        def _(pe):

            def qkv_slot(j, q, r):
                pe.wait_ge(R.split, 2 * q + r + 1)
                for t in range(NB):
                    if past(j, 1):
                        pe.wait_ge(R.tile_free, NB * (j - 1) + t + 1)
                    for k in range(KT):
                        w = slice(k * SLOT, k * SLOT + SLOT)
                        tk = slice(P * t, P * t + P)
                        out = bank[:, 4 + t, 0:SLOT]
                        if isinstance(j, int) and j == 0 and t == 0:
                            pe.wait_ge(u_done, k + 1)
                        nc.tensor.matmul(out, u_hi[:, k, tk], R.hi[:, r, w], start=k == 0, stop=False)
                        nc.tensor.matmul(out, u_lo[:, k, tk], R.hi[:, r, w], start=False, stop=False)
                        last = nc.tensor.matmul(out, u_hi[:, k, tk], R.lo[:, r, w], start=False, stop=k == KT - 1)
                    last.then_inc(R.tile_done, 1)

            each_slot(pe, qkv, qkv_slot)
            outs = [[(bank[:, b, :], slice(0, GRID))] for b in range(4)]
            each_slot(pe, mixed, lambda j, q, r: gemm_slot(pe, nc, R, mixed, j, q, r, u_hi, u_lo, outs))
            for t in range(NB):
                pe.wait_ge(roped, RN * (t + 1))
                if t >= 2:
                    pe.wait_ge(tq_read, 2 * (t - 1))
                elif t == 0:
                    pe.wait_ge(R.tile_free, mixed.end())
                for j in range(4):
                    nc.tensor.transpose(bank[:, 4 + 2 * (t % 2), j * P:j * P + P], tok[:, t, j * P:j * P + P], C("ident"))
                nc.tensor.transpose(bank[:, 5 + 2 * (t % 2), 0:P], tok[:, t, 512:640], C("ident")).then_inc(tq, 1)
            pe.wait_ge(tq_read, 2 * NB)

            def scores(i):
                hh, n = divmod(i, NB)
                ks, c0 = keys(n)
                if i >= 2:
                    pe.wait_ge(s_read, i - 1)
                hp = slice(64 * (hh // 4), 64 * (hh // 4) + 64)
                nc.tensor.matmul(bank[:, 4 + i % 2, c0:3 * P], q_t[hp, hh % 4, P * n:P * n + P],
                                 k_t[hp, P * ks[0]:P * ks[-1] + P], start=True, stop=True).then_inc(s_done, 1)

            def turn(i):
                ks, c0 = keys(i % NB)
                pe.wait_ge(p_done, i + 1)
                if i >= 2:
                    pe.wait_ge(pt_copied, i - 1)
                for b in range(len(ks)):
                    c = c0 + P * b
                    last = nc.tensor.transpose(bank[:, i % 2, c:c + P], s[:, i % 2, c:c + P], C("ident"))
                last.then_inc(t_done, 1)

            def values(i):
                ks, c0 = keys(i % NB)
                pe.wait_ge(pt_copied, i + 1)
                if i >= 2:
                    pe.wait_ge(o_read, i - 1)
                for b, kb in enumerate(ks):
                    c = c0 + P * b
                    last = nc.tensor.matmul(bank[:, 2 + i % 2, 0:P], pt[:, i % 2, c:c + P], tok[:, kb, 640:768],
                                            start=b == 0, stop=b == len(ks) - 1)
                last.then_inc(o_done, 1)

            scores(0)
            for i in range(NI):
                if i + 1 < NI:
                    scores(i + 1)
                turn(i)
                if i >= 1:
                    values(i - 1)
            values(NI - 1)
            pe.wait_ge(o_read, NI)
            for t in range(NB):
                if t >= 2:
                    pe.wait_ge(ta_read, t - 1)
                for f in range(4):
                    last = nc.tensor.transpose(bank[:, 6 + t % 2, f * P:f * P + P], tok[:, t, f * P:f * P + P], C("ident"))
                last.then_inc(ta, 1)

        @block.scalar
        def _(act):
            for k in range(KT):
                if k == 4:
                    hi_slot(act, nc, R, 0, 0, None)
                act.wait_ge(normed, k + 1)
                nc.scalar.activation(u_hi[:, k, :], tmp[:, 4 + k % 4, :], ACT.Copy).then_inc(u_hi_done, 1)

            def qkv_slot(j, q, r):
                hi_next(act, nc, R, qkv, j, q, r)
                for t in range(NB):
                    act.wait_ge(R.tile_done, NB * j + t + 1)
                    nc.scalar.activation(tok[:, t, bass.ds(SLOT * j, SLOT)], bank[:, 4 + t, 0:SLOT], ACT.Copy).then_inc(R.tile_free, 1)

            each_slot(act, qkv, qkv_slot)
            for t in range(NB):
                act.wait_ge(R.tile_free, qkv.end())
                act.wait_ge(u_done, KT)
                if t >= 2:
                    act.wait_ge(hsum, t - 1)
                nc.scalar.activation(tmp[:, 4 + 2 * (t % 2):6 + 2 * (t % 2), :].rearrange("p a b -> p (a b)")[:, 0:640],
                                     tok[:, t, 0:640], ACT.Square).then_inc(hsq, 1)
            act.wait_ge(hsum, NB)
            nc.scalar.activation(hs, hs, ACT.Sqrt, scale=1.0 / HD, bias=EPS).then_inc(hstd, 1)
            act.wait_ge(mu_done, 2)
            act.wait_ge(edges, 2)

            def mixed_slot(j, q, r):
                hi_next(act, nc, R, mixed, j, q, r)
                for m in range(2):
                    t = 2 * j + m
                    b = (r * 2 + m) % 4
                    act.wait_ge(R.tile_done, mixed.c0 + t + 1)
                    if t >= 2:
                        act.wait_ge(pairs_sum, t - 1)
                    nc.scalar.activation(shift[:, m, 1:GRID + 1], bank[:, b, :], ACT.Copy).then_inc(taken, 1)
                    nc.scalar.activation(zr[:, t, :], bank[:, b, :], ACT.Copy, scale=mu[:, 0, t:t + 1]).then_inc(R.tile_free, 1)

            each_slot(act, mixed, mixed_slot)
            for t in range(NB):
                act.wait_ge(tq, t + 1)
                nc.scalar.activation(q_t[:, :, P * t:P * t + P], bank[:, 4 + 2 * (t % 2), :].rearrange("p (a b) -> p a b", a=4),
                                     ACT.Copy, scale=0.125).then_inc(tq_read, 1)
                nc.scalar.activation(k_t[:, P * t:P * t + P], bank[:, 5 + 2 * (t % 2), 0:P], ACT.Copy).then_inc(tq_read, 1)

            def read_o(i):
                hh, n = divmod(i, NB)
                act.wait_ge(o_done, i + 1)
                act.wait_ge(r_done, i + 1)
                at = 64 * (hh // 4)
                nc.scalar.activation(tok[:, n, hh * HD:hh * HD + HD], bank[:, 2 + i % 2, at:at + HD], ACT.Copy,
                                     scale=rden[:, i:i + 1]).then_inc(o_read, 1)

            for i in range(NI):
                hh, n = divmod(i, NB)
                c0 = keys(n)[1]
                if i >= 2:
                    act.wait_ge(t_done, i - 1)
                nc.scalar.activation(s[:, i % 2, 3 * P:3 * P + 1], sinks[:, hh:hh + 1], ACT.Copy).then_inc(s_sink, 1)
                act.wait_ge(mx_done, i + 1)
                nc.scalar.activation(s[:, i % 2, c0:], s[:, i % 2, c0:], ACT.Exp, bias=nm[:, i % 2:i % 2 + 1],
                                     accum_out=den[:, i:i + 1]).then_inc(p_done, 1)
                if i >= 2:
                    read_o(i - 2)
            read_o(NI - 2)
            read_o(NI - 1)
            for t in range(NB):
                act.wait_ge(ta, t + 1)
                nc.scalar.activation(attn_t[:, :, P * t:P * t + P], bank[:, 6 + t % 2, :].rearrange("p (a b) -> p a b", a=4),
                                     ACT.Copy).then_inc(ta_read, 1)

        @block.vector
        def _(dve):
            m0 = PARAMS["mu"][0]
            nc.vector.tensor_scalar(mu[:, 0, :], PV[:, m0:m0 + 14], -1.0, 1.0, ALU.mult, ALU.add).then_inc(mu_done, 1)
            nc.vector.tensor_scalar(mu[:, 1, :], PV[:, m0:m0 + 14], 0.5, None, ALU.mult).then_inc(mu_done, 1)
            nc.vector.memset(shift[:, :, 0:1], 0.0).then_inc(edges, 1)
            nc.vector.memset(shift[:, :, GRID + 1:GRID + 2], 0.0).then_inc(edges, 1)
            nc.vector.reciprocal(rs, rs).then_inc(rs_done, 1)
            dve.wait_ge(rs_done, 1)
            for k in range(KT + 1):
                if k < KT:
                    if k >= 4:
                        dve.wait_ge(u_done, k - 3)
                    nc.vector.scalar_tensor_tensor(tmp[:, 4 + k % 4, :], x[:, k, :], gain("mix2", k), rs, ALU.mult, ALU.mult).then_inc(normed, 1)
                if k:
                    dve.wait_ge(u_hi_done, k)
                    nc.vector.tensor_tensor(u_lo[:, k - 1, :], tmp[:, 4 + (k - 1) % 4, :], u_hi[:, k - 1, :].bitcast(F32),
                                            ALU.subtract).then_inc(u_done, 1)
                if k == 3:
                    lo_slot(dve, nc, R, 0, 0)
            each_slot(dve, qkv, lambda j, q, r: lo_next(dve, nc, R, qkv, j, q, r))
            dve.wait_ge(small, 64)
            for t in range(NB):
                dve.wait_ge(hsq, t + 1)
                src = tmp[:, 4 + 2 * (t % 2):6 + 2 * (t % 2), :].rearrange("p a b -> p (a b)")[:, 0:640]
                nc.vector.tensor_reduce(hs[:, t, :], src.rearrange("p (a b) -> p a b", a=10), X, ALU.add).then_inc(hsum, 1)
            dve.wait_ge(hstd, 1)
            nc.vector.reciprocal(hs, hs).then_inc(hrs, 1)
            dve.wait_ge(hrs, 1)

            def rotate(t):
                nc.vector.tensor_tensor(qk(t), qk(t), hs[:, t, :].unsqueeze(2).broadcast_to([P, 10, HD]), ALU.mult).then_inc(hn, 1)
                dve.wait_ge(hn, 2 * t + 1)
                nc.vector.tensor_tensor(qk(t), qk(t), heads[:], ALU.mult).then_inc(hn, 1)
                dve.wait_ge(hn, 2 * t + 2)
                x1, x2 = qk(t)[:, :, 0:ROT], qk(t)[:, :, ROT:2 * ROT]
                if t:
                    dve.wait_ge(roped, RN * t)
                for at, a, b in ((0, x1, cos(t)), (1, x2, sin(t)), (2, x2, cos(t)), (3, x1, sin(t))):
                    nc.vector.tensor_tensor(rope[:, at], a, b, ALU.mult).then_inc(roped, 1)
                dve.wait_ge(roped, RN * t + 4)
                nc.vector.tensor_tensor(x1, rope[:, 0], rope[:, 1], ALU.subtract).then_inc(roped, 1)
                nc.vector.tensor_tensor(x2, rope[:, 2], rope[:, 3], ALU.add).then_inc(roped, 1)

            def mixed_slot(j, q, r):
                lo_next(dve, nc, R, mixed, j, q, r)
                if j < NB:
                    rotate(j)
                for m in range(2):
                    t = 2 * j + m
                    dve.wait_ge(taken, t + 1)
                    if t >= 1:
                        dve.wait_ge(shifted, t)
                    nc.vector.tensor_tensor(tmp[:, t % 2, :], shift[:, m, 0:GRID], shift[:, m, 2:GRID + 2], ALU.add).then_inc(pairs_sum, 1)
                    dve.wait_ge(pairs_sum, t + 1)
                    dve.wait_ge(R.tile_free, mixed.c0 + t + 1)
                    nc.vector.scalar_tensor_tensor(zr[:, t, :], tmp[:, t % 2, :], mu[:, 1, t:t + 1], zr[:, t, :],
                                                   ALU.mult, ALU.add).then_inc(shifted, 1)

            each_slot(dve, mixed, mixed_slot)

            def copy_pt(i):
                c0 = keys(i % NB)[1]
                dve.wait_ge(p_done, i + 1)
                nc.vector.reciprocal(rden[:, i:i + 1], den[:, i:i + 1]).then_inc(r_done, 1)
                dve.wait_ge(t_done, i + 1)
                if i >= 2:
                    dve.wait_ge(o_done, i - 1)
                nc.vector.tensor_copy(pt[:, i % 2, c0:], bank[:, i % 2, c0:3 * P]).then_inc(pt_copied, 1)

            for i in range(NI):
                hh, n = divmod(i, NB)
                ks, c0 = keys(n)
                b0 = P * (ks[0] - n + 1)
                dve.wait_ge(s_done, i + 1)
                if i >= 2:
                    dve.wait_ge(t_done, i - 1)
                nc.vector.tensor_tensor(s[:, i % 2, c0:3 * P], bank[:, 4 + i % 2, c0:3 * P],
                                        const2("band")[:, b0:b0 + P * len(ks)], ALU.add).then_inc(s_read, 1)
                dve.wait_ge(s_read, i + 1)
                dve.wait_ge(s_sink, i + 1)
                nc.vector.tensor_reduce(nm[:, i % 2:i % 2 + 1], s[:, i % 2, c0:], X, ALU.max, negate=True).then_inc(mx_done, 1)
                if i >= 1:
                    copy_pt(i - 1)
            copy_pt(NI - 1)


def rwkv_block(nc, io, C, PV, zr, rw_t):
    with ExitStack() as ctx:
        def sem(name):
            return nc.alloc_semaphore(f"r_{name}")

        def sb(name, shape, dt=F32):
            return ctx.enter_context(nc.sbuf_tensor(f"r_{name}", shape, dt))

        def column(name, k=0):
            at = PARAMS[name][0] + k
            return PV[:, at:at + 1]

        NU = 2 * RW_FI
        unit = lambda u: (u // 2, u % 2)
        KAPPA = float(np.exp(-0.5))
        levels = sb("levels", [P, 2, LEVELS, P], U8)
        reset = sb("reset", [P, GRID])
        lora = sb("lora", [P, 2, GRID])
        ka1 = sb("ka1", [P, RW_FI])
        sg, rate, cum, before = (sb(n, [P, GRID]) for n in ("sg", "rate", "cum", "before"))
        e_neg, kdir = sb("e_neg", [P, GRID]), sb("kdir", [P, GRID])
        e_pos = cum
        bz = sb("bz", [P, 2, GRID])
        lora_g = kdir[:]
        r_s, a_s, b_s, k_s = (sb(n, [P, 2, GRID]) for n in ("r_s", "a_s", "b_s", "k_s"))
        b_tm, k_tm = sb("b_tm", [P, 2, NB, P]), sb("k_tm", [P, 2, NB, P])
        v_tm = sb("v_tm", [P, 2, NB, P])
        wr = sb("wr", [P, 2, 2, NB, P])
        level_in = wr[:].rearrange("p d h t f -> p (d h t f)")[:, 0:2 * LEVELS * P]
        ab_t, rb_t, ak_t, rk_t = (sb(n, [P, 2, NB, P]) for n in ("ab_t", "rb_t", "ak_t", "rk_t"))
        x, x_t, z = (sb(n, [P, 2, NB, P]) for n in ("x", "x_t", "z"))
        wu = sb("wu", [P, 2, NB, 2, HD])
        gi = sb("gi", [P, NCH, NU, P])
        s = sb("s", [P, NCH, NU, HD])
        pc = sb("pc", [P, NCH, NU])
        stat = reset[:, 0:16 * NB].rearrange("p (a b c) -> p a b c", a=2, b=NB)
        bank = ctx.enter_context(nc.psum_tensor("r_bank", [P, 8, 512], F32))

        in_loaded, reset_done, tanh_done, sqk, ksum, kstd, kmax, krec, kk_done, ka1_done, gate_sig = (
            sem(n) for n in ("in_loaded", "reset_done", "tanh_done", "sqk", "ksum", "kstd", "kmax", "krec", "kk_done",
                             "ka1_done", "gate_sig"))
        levels_loaded, gate_loaded, levels_done = sem("levels_loaded"), sem("gate_loaded"), sem("levels_done")
        side_done, side_read, summed, c_done, e_done, kd1, kd_done, tt_done, bonus_done = (
            sem(n) for n in ("side_done", "side_read", "summed", "c_done", "e_done", "kd1", "kd_done", "tt_done", "bonus_done"))
        a_done, a_read, x_init, z_done, z_read, pr_done, cp_done = (
            sem(n) for n in ("a_done", "a_read", "x_init", "z_done", "z_read", "pr_done", "cp_done"))
        wu_done, wu_read, rp_done, rp_read, y0_done, y0_read, g_done, g_mask, g_read, d_done, d_read = (
            sem(n) for n in ("wu_done", "wu_read", "rp_done", "rp_read", "y0_done", "y0_read",
                             "g_done", "g_mask", "g_read", "d_done", "d_read"))
        step_done, step_add, state_done, y_done, y_sum, mean, centred, ysq, var, gstd, grs, yn, yt, scaled, gl_done, with_bonus, rw_done = (
            sem(n) for n in ("step_done", "step_add", "state_done", "y_done", "y_sum", "mean", "centred", "ysq", "var",
                             "gstd", "grs", "yn", "yt", "scaled", "gl_done", "with_bonus", "rw_done"))

        tiles = lambda a: a.rearrange("p (a b) -> p a b", a=NB)
        tile = lambda a, t: a[:, t * P:t * P + P]
        four = lambda m: m.unsqueeze(1).broadcast_to([P, NB, P])
        chunked = lambda a: a.rearrange("p (c n) -> p c n", c=NCH)
        hp = lambda hh: slice(64 * hh, 64 * hh + 64)
        level = lambda side, k: four(levels[:, side, k, :])
        R_, K_, V_ = 0, RW_FI, 2 * RW_FI
        SIDE, AN, PR = 7, 10, 18
        NZ = 2 * (LEVELS - 1)

        def pr_at(u, k, hh, of_t):
            return PR * u + (4 * (k - 1) + 2 * hh + of_t + 1 if k < LEVELS - 1 else 16 + hh + 1)

        block = ctx.enter_context(nc.Block())

        @block.sync
        def _(sp):
            sp.dma_start(lora[0:64], io["lora_w"].rearrange("d p n -> p d n")).then_inc(in_loaded, 16)
            sp.dma_start(lora[64:128], io["lora_a"].rearrange("d p n -> p d n")).then_inc(in_loaded, 16)
            sp.dma_start(level_in, io["levels"]).then_inc(levels_loaded, 16)
            sp.wait_ge(tt_done, 4 * NU)
            sp.dma_start(lora_g, io["lora_g"]).then_inc(gate_loaded, 16)

        @block.tensor
        def _(pe):
            def side(n):
                if n >= 2:
                    pe.wait_ge(side_read, n - 1)
                return bank[:, 6 + n % 2, :]

            def lora_products(u):
                fi, d = unit(u)
                nc.tensor.matmul(side(SIDE * u), lora[0:64, d, fi * P:fi * P + P], zr[0:64, 12, :], start=True, stop=True).then_inc(side_done, 1)
                nc.tensor.matmul(side(SIDE * u + 1), lora[64:128, d, fi * P:fi * P + P], zr[64:128, 12, :], start=True, stop=True).then_inc(side_done, 1)

            def turn(u):
                fi, d = unit(u)
                pe.wait_ge(tt_done, 4 * (u + 1))
                for k, src in enumerate((a_s[:, d], b_s[:, d], k_s[:, d], zr[:, V_ + fi, :])[0:4 - d]):
                    out = side(SIDE * u + 2 + k)
                    for t in range(NB):
                        last = nc.tensor.transpose(tile(out, t), tile(src, t), C("ident"))
                    last.then_inc(side_done, 1)
                if d == 1:
                    out = side(SIDE * u + 5)
                    nc.tensor.matmul(out, C("head_ones"), bz[:, 0, :], start=True, stop=False)
                    nc.tensor.matmul(out, C("head_ones"), bz[:, 1, :], start=False, stop=True).then_inc(side_done, 1)

            def attention(u):
                fi, d = unit(u)
                pe.wait_ge(tt_done, 4 * (u + 1))
                if u:
                    pe.wait_ge(y0_read, u)
                    pe.wait_ge(g_read, 2 * u)
                    pe.wait_ge(d_read, 4 * u)
                    pe.wait_ge(rp_read, u)
                kinds = ((b_s, a_s, 4), (a_s, b_s, 2), (b_s, r_s, 0), (k_s, a_s, 4), (k_s, r_s, 2))
                for m, (left, right, b) in enumerate(kinds):
                    for hh in range(2):
                        if m >= 3:
                            pe.wait_ge(a_read, AN * u + 2 * (m - 3) + hh + 1)
                        for t in range(NB):
                            tk = slice(P * t, P * t + P)
                            last = nc.tensor.matmul(bank[:, b + hh, tk], left[hp(hh), d, tk], right[hp(hh), d, tk], start=True, stop=True)
                        last.then_inc(a_done, 1)

            def double(u, k):
                for hh in range(2):
                    if k == 1:
                        pe.wait_ge(a_read, AN * u + 6)
                    else:
                        pe.wait_ge(cp_done, pr_at(u, k - 1, hh, 1))
                        pe.wait_ge(z_read, NZ * u + 2 * (k - 2) + hh + 1)
                    for t in range(NB):
                        last = nc.tensor.matmul(tile(bank[:, hh, :], t), ab_t[:, hh, t, :], x[:, hh, t, :], start=True, stop=True)
                    last.then_inc(z_done, 1)
                for hh in range(2):
                    if k == 1:
                        pe.wait_ge(a_read, AN * (u + 1))
                    pe.wait_ge(z_read, NZ * u + 2 * (k - 1) + hh + 1)
                    if k < LEVELS - 1:
                        for t in range(NB):
                            last = nc.tensor.matmul(tile(bank[:, 2 + hh, :], t), x_t[:, hh, t, :], z[:, hh, t, :], start=True, stop=True)
                        last.then_inc(pr_done, 1)
                    for t in range(NB):
                        last = nc.tensor.matmul(tile(bank[:, 4 + hh, :], t), z[:, hh, t, :], x_t[:, hh, t, :], start=True, stop=True)
                    last.then_inc(pr_done, 1)

            def keys_values(u):
                fi, d = unit(u)
                out = side(SIDE * u + 6)
                for hh in range(2):
                    for t in range(NB):
                        at = (hh * NB + t) * HD
                        last = nc.tensor.matmul(out[:, at:at + HD], ak_t[:, hh, t, :], v_tm[:, fi % 2, t, hh * HD:hh * HD + HD],
                                                start=True, stop=True)
                last.then_inc(side_done, 1)

            def late(u):
                fi, d = unit(u)
                pe.wait_ge(side_read, SIDE * (u + 1))
                for hh in range(2):
                    pe.wait_ge(cp_done, PR * (u + 1) - 1 + hh)
                    for t in range(NB):
                        last = nc.tensor.matmul(tile(bank[:, 2 + hh, :], t), x_t[:, hh, t, :], wr[:, d, hh, t, :], start=True, stop=True)
                    last.then_inc(wu_done, 1)
                if u + 1 < NU:
                    turn(u + 1)
                pe.wait_ge(wu_read, 2 * (u + 1))
                for hh in range(2):
                    for t in range(NB):
                        last = nc.tensor.matmul(bank[hp(hh), 1, t * P:t * P + P], wu[:, 0, t, hh, :], rb_t[:, hh, t, :], start=True, stop=True)
                last.then_inc(rp_done, 1)
                for hh in range(2):
                    for t in range(NB):
                        out = bank[:, 4, t * P + hh * HD:t * P + hh * HD + HD]
                        nc.tensor.matmul(out, rb_t[:, hh, t, :], wu[:, 1, t, hh, :], start=True, stop=False)
                        last = nc.tensor.matmul(out, rk_t[:, hh, t, :], v_tm[:, fi % 2, t, hh * HD:hh * HD + HD], start=False, stop=True)
                last.then_inc(y0_done, 1)
                for half in range(2):
                    rr = hp(half)
                    for t in range(NB):
                        w = wu[rr, 0, t].rearrange("p a b -> p (a b)")
                        last = nc.tensor.matmul(tile(bank[:, 5 - 5 * half, :], t), w, b_tm[rr, d, t, :], start=True, stop=True)
                    last.then_inc(g_done, 1)
                for half in range(2):
                    rr = hp(half)
                    for t in range(NB):
                        u0 = wu[rr, 1, t].rearrange("p a b -> p (a b)")
                        nc.tensor.matmul(tile(bank[:, 2 + half, :], t), b_tm[rr, d, t, :], u0, start=True, stop=False)
                        last = nc.tensor.matmul(tile(bank[:, 2 + half, :], t), k_tm[rr, d, t, :], v_tm[rr, fi % 2, t, :], start=False, stop=True)
                    last.then_inc(d_done, 1)

            for fi in range(RW_FI):
                pe.wait_ge(sqk, fi + 1)
                nc.tensor.matmul(bank[:, fi, :], C("head_ones"), bz[:, fi % 2, :], start=True, stop=True).then_inc(ksum, 1)
            pe.wait_ge(in_loaded, 32)
            pe.wait_ge(tanh_done, 1)
            lora_products(0)
            turn(0)
            for u in range(NU):
                attention(u)
                for k in range(1, LEVELS):
                    double(u, k)
                    if k == 1:
                        keys_values(u)
                        if u + 1 < NU:
                            lora_products(u + 1)
                late(u)
            pe.wait_ge(y0_read, NU)
            pe.wait_ge(g_read, 2 * NU)
            pe.wait_ge(d_read, 4 * NU)
            for step in range(1, NCH - 1):
                for d in range(2):
                    pe.wait_ge(state_done, 2 * (step - 1) + d + 1)
                    c, front = (step, step - 1) if d == 0 else (NCH - 1 - step, NCH - step)
                    for fi in range(RW_FI):
                        last = nc.tensor.matmul(bank[:, d, fi * HD:fi * HD + HD], gi[:, c, 4 * d + fi, :], s[:, front, 4 * d + fi, :],
                                                start=True, stop=True)
                    last.then_inc(step_done, 1)
            pe.wait_ge(state_done, 2 * (NCH - 1))
            pe.wait_ge(rp_read, NU)
            for t in range(NB):
                if t >= 2:
                    pe.wait_ge(y_sum, 2 * (t - 1))
                for half in range(2):
                    c = 2 * t + half
                    tk = slice(CH * c, CH * c + CH)
                    dirs = [(d, f) for d, f in ((0, c - 1), (1, c + 1)) if 0 <= f < NCH]
                    for fi in range(RW_FI):
                        for par in range(2):
                            for d, f in dirs:
                                last = nc.tensor.matmul(bank[hp(half), 2 + 2 * (t % 2) + par, fi * HD:fi * HD + HD],
                                                        zr[hp(par), (R_, K_)[d] + fi, tk], s[hp(par), f, 4 * d + fi, :],
                                                        start=(d, f) == dirs[0], stop=(d, f) == dirs[-1])
                last.then_inc(y_done, 1)
            pe.wait_ge(gate_sig, 1)
            pe.wait_ge(gate_loaded, 16)
            pe.wait_ge(yn, NB)
            for fi in range(RW_FI):
                if fi >= 2:
                    pe.wait_ge(scaled, fi - 1)
                    pe.wait_ge(rw_done, fi - 1)
                for t in range(NB):
                    last = nc.tensor.transpose(tile(bank[:, 6 + fi % 2, :], t), tile(zr[:, V_ + fi, :], t), C("ident"))
                last.then_inc(yt, 1)
                nc.tensor.matmul(bank[:, fi % 2, :], lora_g[:, fi * P:fi * P + P], zr[:, 13, :], start=True, stop=True).then_inc(gl_done, 1)

        @block.scalar
        def _(act):
            def rates(u):
                fi, d = unit(u)
                if u:
                    act.wait_ge(tt_done, 4 * u)
                act.wait_ge(side_done, SIDE * u + 1)
                nc.scalar.activation(sg[:], bank[:, 6 + SIDE * u % 2, :], ACT.Sigmoid, bias=column("w0", 4 * d + fi)).then_inc(side_read, 1)
                act.wait_ge(side_done, SIDE * u + 2)
                nc.scalar.activation(rate[:], bank[:, 7 - SIDE * u % 2, :], ACT.Sigmoid, bias=column("a0", 4 * d + fi)).then_inc(side_read, 1)

            def decays(u):
                act.wait_ge(c_done, u + 1)
                nc.scalar.activation(e_neg[:], cum[:], ACT.Exp, scale=KAPPA).then_inc(e_done, 1)
                nc.scalar.activation(e_pos[:], cum[:], ACT.Exp, scale=-KAPPA).then_inc(e_done, 1)
                nc.scalar.activation(before[:], before[:], ACT.Exp, scale=-KAPPA).then_inc(e_done, 1)

            def token_major(u):
                fi, d = unit(u)
                n = SIDE * u
                act.wait_ge(levels_done, 1)
                act.wait_ge(side_done, n + 3)
                nc.scalar.activation(wr[:, d, :, :, 0:HD].rearrange("p h t f -> p t h f"),
                                     bank[:, 6 + n % 2, :].rearrange("p (t h f) -> p t h f", t=NB, h=2), ACT.Copy).then_inc(side_read, 1)
                last = (v_tm[:, fi % 2].rearrange("p a b -> p (a b)") if d == 0 else bz[:, 0, :])
                for k, dst in ((3, b_tm[:, d].rearrange("p a b -> p (a b)")), (4, k_tm[:, d].rearrange("p a b -> p (a b)")), (5, last)):
                    act.wait_ge(side_done, n + k + 1)
                    nc.scalar.activation(dst, bank[:, 6 + (n + k) % 2, :], ACT.Copy).then_inc(side_read, 1)

            def keys_values(u):
                n = SIDE * u + 6
                act.wait_ge(side_done, n + 1)
                nc.scalar.activation(wr[:, u % 2, :, :, HD:P], bank[:, 6 + n % 2, :].rearrange("p (h t f) -> p h t f", h=2, t=NB),
                                     ACT.Copy).then_inc(side_read, 1)

            def late(u):
                fi, d = unit(u)
                for hh in range(2):
                    act.wait_ge(wu_done, 2 * u + hh + 1)
                    nc.scalar.activation(wu[:, :, :, hh, :].rearrange("p k t f -> p t k f"),
                                         bank[:, 2 + hh, :].rearrange("p (t k f) -> p t k f", t=NB, k=2), ACT.Copy).then_inc(wu_read, 1)
                if u + 1 < NU:
                    token_major(u + 1)
                for half in range(2):
                    act.wait_ge(d_done, 2 * u + half + 1)
                    for hh in range(2):
                        nc.scalar.activation(s[hp(hh), half::2, 4 * d + fi, :],
                                             tiles(bank[hp(hh), 2 + half, :])[:, :, hh * HD:hh * HD + HD], ACT.Copy).then_inc(d_read, 1)

            nc.scalar.activation(zr[0:64, 12, :], zr[0:64, 12, :], ACT.Tanh).then_inc(tanh_done, 1)
            for fi in range(RW_FI):
                if fi >= 2:
                    act.wait_ge(ksum, fi - 1)
                nc.scalar.activation(bz[:, fi % 2, :], zr[:, K_ + fi, :], ACT.Square, scale=column("k_k", fi)).then_inc(sqk, 1)
            for fi in range(RW_FI):
                act.wait_ge(ksum, fi + 1)
                nc.scalar.activation(rw_t[:, fi, :], bank[:, fi, :], ACT.Sqrt).then_inc(kstd, 1)
            rates(0)
            nc.scalar.activation(zr[:, 13, :], zr[:, 13, :], ACT.Sigmoid).then_inc(gate_sig, 1)
            decays(0)
            token_major(0)
            for u in range(NU):
                if u:
                    act.wait_ge(wu_done, 2 * u)
                for hh in range(2):
                    nc.scalar.activation(x_t[:, hh], four(C("ident")), ACT.Copy).then_inc(x_init, 1)
                for hh in range(2):
                    nc.scalar.activation(x[:, hh], four(C("ident")), ACT.Copy).then_inc(x_init, 1)
                for k in range(1, LEVELS):
                    for hh in range(2):
                        act.wait_ge(z_done, NZ * u + 2 * (k - 1) + hh + 1)
                        nc.scalar.activation(z[:, hh].rearrange("p a b -> p (a b)"), bank[:, hh, :], ACT.Copy).then_inc(z_read, 1)
                    if k == 1:
                        keys_values(u)
                    if u + 1 < NU:
                        if k == 1:
                            rates(u + 1)
                        elif k == 3:
                            decays(u + 1)
                late(u)
            for t in range(NB):
                act.wait_ge(centred, t + 1)
                if t >= 2:
                    act.wait_ge(var, t - 1)
                nc.scalar.activation(tiles(bz[:, t % 2, :]), zr[:, V_:V_ + RW_FI, t * P:t * P + P], ACT.Square).then_inc(ysq, 1)
            act.wait_ge(var, NB)
            nc.scalar.activation(stat[:, 1], stat[:, 1], ACT.Sqrt, scale=1.0 / HD, bias=GN_EPS).then_inc(gstd, 1)
            for fi in range(RW_FI):
                act.wait_ge(yt, fi + 1)
                if fi >= 2:
                    act.wait_ge(rw_done, fi - 1)
                nc.scalar.activation(bz[:, fi % 2, :], bank[:, 6 + fi % 2, :], ACT.Identity, scale=column("lnx_w", fi),
                                     bias=column("lnx_b", fi)).then_inc(scaled, 1)

        @block.vector
        def _(dve):
            def sums(u):
                fi, d = unit(u)
                dve.wait_ge(side_read, SIDE * u + 1)
                if u:
                    dve.wait_ge(e_done, 3 * u)
                nc.vector.tensor_tensor_scan(cum[:], reset[:], sg[:], 0.0, ALU.mult, ALU.add).then_inc(summed, 1)
                dve.wait_ge(summed, 3 * fi + d + 1)
                if d == 0:
                    nc.vector.tensor_tensor(before[:], cum[:], sg[:], ALU.subtract).then_inc(c_done, 1)
                else:
                    total = chunked(cum[:])[:, :, CH - 1:CH].broadcast_to([P, NCH, CH])
                    nc.vector.tensor_tensor(chunked(before[:]), total, chunked(cum[:]), ALU.subtract).then_inc(summed, 1)
                    dve.wait_ge(summed, 3 * fi + 3)
                    nc.vector.tensor_tensor(cum[:], before[:], sg[:], ALU.add).then_inc(c_done, 1)

            def directed(u):
                fi, d = unit(u)
                dve.wait_ge(side_read, SIDE * u + 2)
                dve.wait_ge(kk_done, fi + 1)
                nc.vector.tensor_scalar(kdir[:], rate[:], column("k_a", fi), ka1[:, fi:fi + 1], ALU.mult, ALU.add).then_inc(kd1, 1)
                dve.wait_ge(kd1, u + 1)
                nc.vector.tensor_tensor(kdir[:], kdir[:], zr[:, K_ + fi, :], ALU.mult).then_inc(kd_done, 1)
                nc.vector.tensor_tensor(rate[:], rate[:], rw_t[:, fi, :], ALU.mult).then_inc(kd_done, 1)

            def scale(u):
                fi, d = unit(u)
                dve.wait_ge(e_done, 3 * (u + 1))
                dve.wait_ge(kd_done, 2 * (u + 1))
                if u and d == 0:
                    dve.wait_ge(bonus_done, u // 2)
                nc.vector.scalar_tensor_tensor(bz[:, d, :], kdir[:], column("r_k", 4 * d + fi), zr[:, R_ + fi, :], ALU.mult, ALU.mult)
                edge = chunked(e_pos[:])[:, :, CH - 1] if d == 0 else chunked(e_pos[:])[:, :, 0]
                nc.vector.tensor_copy(pc[:, :, 4 * d + fi], edge)
                nc.vector.scalar_tensor_tensor(a_s[:, d, :], rw_t[:, fi, :], -1.0, before[:], ALU.mult, ALU.mult).then_inc(tt_done, 1)
                nc.vector.tensor_tensor(b_s[:, d, :], rate[:], e_neg[:], ALU.mult).then_inc(tt_done, 1)
                nc.vector.tensor_tensor(k_s[:, d, :], kdir[:], e_neg[:], ALU.mult).then_inc(tt_done, 1)
                nc.vector.tensor_tensor(r_s[:, d, :], zr[:, R_ + fi, :], e_pos[:], ALU.mult).then_inc(tt_done, 1)

            def bonus(u):
                fi, d = unit(u)
                dve.wait_ge(side_read, SIDE * u + 6)
                nc.vector.tensor_tensor(rw_t[:, fi, :], bz[:, 0, :], zr[:, V_ + fi, :], ALU.mult).then_inc(bonus_done, 1)

            def attention(u):
                fi, d = unit(u)
                dve.wait_ge(x_init, 4 * (u + 1))
                dve.wait_ge(levels_done, 1)
                strict, incl = (C("lt"), C("le")) if d == 0 else (C("gt"), C("ge"))
                n = AN * u
                for hh in range(2):
                    dve.wait_ge(a_done, n + hh + 1)
                    nc.vector.tensor_tensor(ab_t[:, hh], tiles(bank[:, 4 + hh, :]), four(strict), ALU.mult)
                    nc.vector.copy_predicated(x_t[:, hh], level(1 - d, 0), tiles(bank[:, 4 + hh, :])).then_inc(a_read, 1)
                for hh in range(2):
                    dve.wait_ge(a_done, n + 3 + hh)
                    nc.vector.copy_predicated(x[:, hh], level(d, 0), tiles(bank[:, 2 + hh, :])).then_inc(a_read, 1)
                for m, (dst, b, mask) in enumerate(((rb_t, 0, incl), (ak_t, 4, strict), (rk_t, 2, incl))):
                    for hh in range(2):
                        dve.wait_ge(a_done, n + 5 + 2 * m + hh)
                        nc.vector.tensor_tensor(dst[:, hh], tiles(bank[:, b + hh, :]), four(mask), ALU.mult).then_inc(a_read, 1)

            def late(u):
                fi, d = unit(u)
                if d == 0:
                    bonus(u + 1)
                dve.wait_ge(rp_done, u + 1)
                nc.vector.tensor_tensor(zr[:, (R_, K_)[d] + fi, :], bank[:, 1, :], r_s[:, d, :], ALU.add).then_inc(rp_read, 1)
                dve.wait_ge(y0_done, u + 1)
                if d == 0:
                    dve.wait_ge(bonus_done, fi + 1)
                    nc.vector.tensor_copy(zr[:, V_ + fi, :], bank[:, 4, :]).then_inc(y0_read, 1)
                else:
                    dve.wait_ge(y0_read, u)
                    nc.vector.tensor_tensor(zr[:, V_ + fi, :], bank[:, 4, :], zr[:, V_ + fi, :], ALU.add).then_inc(y0_read, 1)
                for half in range(2):
                    g = gi[:, half::2, 4 * d + fi, :]
                    dve.wait_ge(g_done, 2 * u + half + 1)
                    nc.vector.tensor_tensor(g, tiles(bank[:, 5 - 5 * half, :]), four(C("head_ones")), ALU.mult).then_inc(g_mask, 1)
                    dve.wait_ge(g_mask, 2 * u + half + 1)
                    nc.vector.tensor_tensor(g, g, four(C("ident")), ALU.add).then_inc(g_read, 1)

            nc.vector.memset(reset[:], 1.0).then_inc(reset_done, 1)
            nc.vector.memset(cum[:], 0.0).then_inc(reset_done, 1)
            dve.wait_ge(reset_done, 2)
            nc.vector.memset(chunked(reset[:])[:, :, 0:1], 0.0).then_inc(reset_done, 1)
            dve.wait_ge(reset_done, 3)
            a0 = PARAMS["k_a"][0]
            nc.vector.tensor_scalar(ka1[:], PV[:, a0:a0 + RW_FI], -1.0, 1.0, ALU.mult, ALU.add).then_inc(ka1_done, 1)
            dve.wait_ge(ka1_done, 1)
            def unit_keys(fi):
                dve.wait_ge(kstd, fi + 1)
                nc.vector.tensor_scalar(rw_t[:, fi, :], rw_t[:, fi, :], 1e-12, None, ALU.max).then_inc(kmax, 1)
                dve.wait_ge(kmax, fi + 1)
                nc.vector.reciprocal(rw_t[:, fi, :], rw_t[:, fi, :]).then_inc(krec, 1)
                dve.wait_ge(krec, fi + 1)
                nc.vector.scalar_tensor_tensor(rw_t[:, fi, :], zr[:, K_ + fi, :], column("k_k", fi), rw_t[:, fi, :],
                                               ALU.mult, ALU.mult).then_inc(kk_done, 1)
            unit_keys(0)
            dve.wait_ge(levels_loaded, 16)
            nc.vector.tensor_copy(levels[:].rearrange("p a b c -> p (a b c)"), level_in).then_inc(levels_done, 1)
            sums(0)
            directed(0)
            scale(0)
            for u in range(NU):
                attention(u)
                for k in range(1, LEVELS):
                    for hh in range(2):
                        if k < LEVELS - 1:
                            dve.wait_ge(pr_done, pr_at(u, k, hh, 0))
                            nc.vector.copy_predicated(x[:, hh], level(u % 2, k), tiles(bank[:, 2 + hh, :])).then_inc(cp_done, 1)
                        dve.wait_ge(pr_done, pr_at(u, k, hh, 1))
                        nc.vector.copy_predicated(x_t[:, hh], level(1 - u % 2, k), tiles(bank[:, 4 + hh, :])).then_inc(cp_done, 1)
                    if u + 1 < NU:
                        if k == 1 and u % 2:
                            unit_keys(u // 2 + 1)
                        elif k == 2:
                            sums(u + 1)
                        elif k == 3:
                            directed(u + 1)
                        elif k == 4:
                            scale(u + 1)
                late(u)
            dve.wait_ge(d_read, 4 * NU)
            dve.wait_ge(rp_read, NU)
            for step in range(NCH - 1):
                for d in range(2):
                    c = step if d == 0 else NCH - 1 - step
                    us = slice(4 * d, 4 * d + 4)
                    at = s[:, c, us, :]
                    if step:
                        dve.wait_ge(step_done, 2 * (step - 1) + d + 1)
                        nc.vector.tensor_tensor(at, bank[:, d, 0:256].rearrange("p (a b) -> p a b", a=4), at, ALU.add).then_inc(step_add, 1)
                        dve.wait_ge(step_add, 2 * (step - 1) + d + 1)
                    nc.vector.tensor_tensor(at, at, pc[:, c, us].unsqueeze(2).broadcast_to([P, 4, HD]), ALU.mult).then_inc(state_done, 1)
            y = lambda t: zr[:, V_:V_ + RW_FI, t * P:t * P + P].rearrange("p a (b c) -> p a b c", b=2)
            per_head = lambda k, t: stat[:, k, t, :].rearrange("p (a b) -> p a b", a=4)
            over_head = lambda k, t: per_head(k, t).unsqueeze(3).broadcast_to([P, 4, 2, HD])
            dve.wait_ge(y0_read, NU)
            for t in range(NB):
                dve.wait_ge(y_done, t + 1)
                for par in range(2):
                    src = bank[:, 2 + 2 * (t % 2) + par, 0:256].rearrange("p (a b) -> p a b", a=4)
                    nc.vector.tensor_tensor(y(t)[:, :, par, :], src, y(t)[:, :, par, :], ALU.add).then_inc(y_sum, 1)
                dve.wait_ge(y_sum, 2 * t + 2)
                nc.vector.tensor_reduce(per_head(0, t), y(t), X, ALU.add).then_inc(mean, 1)
                dve.wait_ge(mean, 2 * t + 1)
                nc.vector.tensor_scalar(stat[:, 0, t, :], stat[:, 0, t, :], 1.0 / HD, None, ALU.mult).then_inc(mean, 1)
                dve.wait_ge(mean, 2 * t + 2)
                nc.vector.tensor_tensor(y(t), y(t), over_head(0, t), ALU.subtract).then_inc(centred, 1)
                dve.wait_ge(ysq, t + 1)
                nc.vector.tensor_reduce(per_head(1, t), tiles(bz[:, t % 2, :]).rearrange("p a (b c) -> p a b c", b=2), X, ALU.add).then_inc(var, 1)
            dve.wait_ge(gstd, 1)
            nc.vector.reciprocal(stat[:, 1], stat[:, 1]).then_inc(grs, 1)
            dve.wait_ge(grs, 1)
            for t in range(NB):
                nc.vector.tensor_tensor(y(t), y(t), over_head(1, t), ALU.mult).then_inc(yn, 1)
            for fi in range(RW_FI):
                dve.wait_ge(scaled, fi + 1)
                nc.vector.tensor_tensor(bz[:, fi % 2, :], bz[:, fi % 2, :], rw_t[:, fi, :], ALU.add).then_inc(with_bonus, 1)
                dve.wait_ge(with_bonus, fi + 1)
                dve.wait_ge(gl_done, fi + 1)
                nc.vector.tensor_tensor(rw_t[:, fi, :], bank[:, fi % 2, :], bz[:, fi % 2, :], ALU.mult).then_inc(rw_done, 1)


def merge_block(nc, io, C, PV, h, attn_t, rw_t, rms):
    with ExitStack() as ctx:
        def sem(name):
            return nc.alloc_semaphore(f"g_{name}")

        def sb(name, shape, dt=F32):
            return ctx.enter_context(nc.sbuf_tensor(f"g_{name}", shape, dt))

        def gain(name, k=0):
            at = PARAMS[name][0] + k
            return PV[:, at:at + 1]

        R = Ring(ctx, nc, "g")
        GROUPS = D_FF2 // D
        gates = R.phase(8)
        up = R.phase(4, 4)
        out = R.phase(4)
        ff1, ff2 = [], []
        for _ in range(GROUPS):
            ff1.append(R.phase(4))
            ff2.append(R.phase(4))
        ple = R.phase(1, 8)
        pgate = R.phase(4)
        x = h[:, :, META:L]
        u_hi, u_lo = sb("u_hi", [P, KT, GRID], F32R), sb("u_lo", [P, KT, GRID], F32R)
        y_hi, y_lo = sb("y_hi", [P, KT, GRID], F32R), sb("y_lo", [P, KT, GRID], F32R)
        branch = sb("branch", [P, 2 * KT, GRID])
        p_raw = sb("p_raw", [P, 2, GRID])
        sq, std, rs = branch[:, 8:10, :], branch[:, 10, :], branch[:, 11, :]
        sq_sum_t = sb("sq_sum", [P, GRID])
        sq_sum = sq_sum_t[:]
        tmp = branch[:, 12:16, :]
        bank = ctx.enter_context(nc.psum_tensor("g_bank", [P, 8, 512], F32))
        whole = slice(0, GRID)
        outs = [[(bank[:, b, :], whole)] for b in range(4)]
        NORMS = ("mix2", "ffn2", "ple")

        sq_added = sem("sq_added")
        squared, summed, std_done, rs_done, normed, u_hi_done, u_done = (
            sem(n) for n in ("squared", "summed", "std_done", "rs_done", "normed", "u_hi_done", "u_done"))
        split_hi, split_lo, both, m_hi, m_done = (
            sem(n) for n in ("split_hi", "split_lo", "both", "m_hi", "m_done"))
        relu_hi, relu_sq, relu_done, p_loaded, p_hi, p_done, ple_gated, x_done, stored = (
            sem(n) for n in ("relu_hi", "relu_sq", "relu_done", "p_loaded", "p_hi", "p_done", "ple_gated", "x_done", "stored"))
        branches = (attn_t, rw_t)
        flat = lambda a, t: a[:, bass.ds(t, 1), :].rearrange("p o n -> p (o n)")

        block = ctx.enter_context(nc.Block())

        @block.sync
        def _(sp):
            load_phase(sp, R, gates, io["w_in2"][10:18])
            sp.dma_start(p_raw[:], io["p"]).then_inc(p_loaded, 16)
            load_phase(sp, R, up, io["w_up"])
            load_phase(sp, R, out, io["w_out"])
            for g in range(GROUPS):
                load_phase(sp, R, ff1[g], io["w_ff1"][4 * g:4 * g + 4])
                load_phase(sp, R, ff2[g], io["w_ff2"][4 * g:4 * g + 4])
            load_phase(sp, R, ple, io["w_ple"])
            load_phase(sp, R, pgate, io["w_ple_gate"])
            for t in range(KT):
                sp.wait_ge(x_done, t + 1)
                sp.dma_start(io["out"][:, t, :], x[:, t, :]).then_inc(stored, 16)
            sp.wait_ge(stored, 16 * KT)

        @block.gpsimd
        def _(pool):
            for n in range(2):
                if n:
                    pool.wait_ge(summed, n)
                add_squares(pool, nc, sq, sq_sum, squared, sq_added, n)

        @block.tensor
        def _(pe):
            def norm(n):
                pe.wait_ge(sq_added, KT * n)
                nc.tensor.matmul(bank[:, 4, :], C("ones"), sq_sum, start=True, stop=True).then_inc(summed, 1)

            def products(ph, hi, lo, rows=range(KT), cols=SLOT, ready=None):
                each_slot(pe, ph, lambda j, q, r: gemm_slot(pe, nc, R, ph, j, q, r, hi, lo, outs, rows, cols, ready))

            products(gates, u_hi, u_lo, ready=(u_done, 0))
            pe.wait_ge(split_lo, 2)
            each_slot(pe, up, lambda j, q, r: gemm_slot(pe, nc, R, up, j, q, r, y_hi, y_lo, outs,
                                                       range(4 * (j // 2), 4 * (j // 2) + 4), 512))
            products(out, u_hi, u_lo, ready=(m_done, 0))
            norm(1)
            for g in range(GROUPS):
                products(ff1[g], u_hi, u_lo, ready=(u_done, KT) if g == 0 else None)
                products(ff2[g], y_hi, y_lo, ready=(relu_done, KT * g))
            pe.wait_ge(p_done, 1)
            products(ple, y_hi, y_lo, range(2), D)
            norm(2)
            products(pgate, u_hi, u_lo, ready=(u_done, 2 * KT))

        @block.scalar
        def _(act):
            def squares(n, ph):
                def tile(t):
                    act.wait_ge(R.tile_free, ph.c0 + t + 1)
                    if t >= 2:
                        act.wait_ge(sq_added, KT * (n - 1) + t - 1)
                    nc.scalar.activation(sq[:, t % 2, :], x[:, t, :], ACT.Square).then_inc(squared, 1)

                def slot(j, q, r):
                    hi_next(act, nc, R, ph, j, q, r)
                    if j >= 1:
                        tile(2 * j - 2)
                        tile(2 * j - 1)

                each_slot(act, ph, slot)
                tile(KT - 2)
                tile(KT - 1)

            def norm(n):
                act.wait_ge(summed, n)
                nc.scalar.activation(std, bank[:, 4, :], ACT.Sqrt, scale=1.0 / D, bias=EPS).then_inc(std_done, 1)

            def norm_hi(n):
                for k in range(KT):
                    if n == 0 and k == 4:
                        hi_slot(act, nc, R, 0, 0, None)
                    act.wait_ge(normed, KT * n + k + 1)
                    nc.scalar.activation(u_hi[:, k, :], tmp[:, k % 4, :], ACT.Copy).then_inc(u_hi_done, 1)

            def weights(ph):
                each_slot(act, ph, lambda j, q, r: hi_next(act, nc, R, ph, j, q, r))

            norm_hi(0)
            for b in range(2):
                nc.scalar.activation(y_hi[:, 4 * b:4 * b + 4, :], branches[b][:], ACT.Copy).then_inc(split_hi, 1)
            act.wait_ge(u_done, KT)

            def gate_slot(j, q, r):
                hi_next(act, nc, R, gates, j, q, r)
                for m in range(2):
                    act.wait_ge(R.tile_done, gates.c0 + 2 * j + m + 1)
                    nc.scalar.activation(flat(branch, 2 * j + m), bank[:, 2 * r + m, :], ACT.Sigmoid).then_inc(R.tile_free, 1)

            each_slot(act, gates, gate_slot)

            def up_slot(j, q, r):
                hi_next(act, nc, R, up, j, q, r)
                if j >= 2:
                    for t in range(4 * (j - 2), 4 * (j - 2) + 4):
                        act.wait_ge(both, t + 1)
                        nc.scalar.activation(u_hi[:, t, :], branch[:, t, :], ACT.Copy).then_inc(m_hi, 1)

            each_slot(act, up, up_slot)
            squares(1, out)
            norm(1)
            norm_hi(1)
            for g in range(GROUPS):
                def relu_slot(j, q, r, g=g):
                    hi_next(act, nc, R, ff1[g], j, q, r)
                    for m in range(2):
                        t = 2 * j + m
                        act.wait_ge(R.tile_done, ff1[g].c0 + t + 1)
                        if KT * g + t >= 4:
                            act.wait_ge(relu_done, KT * g + t - 3)
                        nc.scalar.activation(branch[:, 4 + t % 4, :], bank[:, (2 * r + m) % 4, :], ACT.Relu).then_inc(R.tile_free, 1)
                        act.wait_ge(R.tile_free, ff1[g].c0 + t + 1)
                        nc.scalar.activation(y_hi[:, t, :], branch[:, 4 + t % 4, :], ACT.Square).then_inc(relu_hi, 1)

                each_slot(act, ff1[g], relu_slot)
                if g < GROUPS - 1:
                    weights(ff2[g])
            squares(2, ff2[-1])
            act.wait_ge(p_loaded, 16)
            nc.scalar.activation(y_hi[:, 0:2, :], p_raw[:], ACT.Copy).then_inc(p_hi, 1)
            weights(ple)
            norm(2)
            norm_hi(2)

            def pgate_slot(j, q, r):
                hi_next(act, nc, R, pgate, j, q, r)
                for m in range(2):
                    t = 2 * j + m
                    act.wait_ge(R.tile_done, pgate.c0 + t + 1)
                    nc.scalar.activation(branch[:, 8 + t, :], bank[:, (2 * r + m) % 4, :], ACT.Sigmoid).then_inc(R.tile_free, 1)

            act.wait_ge(u_done, 3 * KT)
            each_slot(act, pgate, pgate_slot)

        @block.vector
        def _(dve):
            def norm(n):
                if n:
                    dve.wait_ge(std_done, n)
                    nc.vector.reciprocal(rs, std).then_inc(rs_done, 1)
                    dve.wait_ge(rs_done, n)
                factor = rs if n else rms[:, META:L]
                for k in range(KT + 1):
                    if k < KT:
                        if k >= 4:
                            dve.wait_ge(u_done, KT * n + k - 3)
                        nc.vector.scalar_tensor_tensor(tmp[:, k % 4, :], x[:, k, :], gain(NORMS[n], k), factor, ALU.mult, ALU.mult).then_inc(normed, 1)
                    if k:
                        dve.wait_ge(u_hi_done, KT * n + k)
                        nc.vector.tensor_tensor(u_lo[:, k - 1, :], tmp[:, (k - 1) % 4, :], u_hi[:, k - 1, :].bitcast(F32),
                                                ALU.subtract).then_inc(u_done, 1)
                    if n == 0 and k == 3:
                        lo_slot(dve, nc, R, 0, 0)

            def add_to_x(ph):
                def slot(j, q, r):
                    lo_next(dve, nc, R, ph, j, q, r)
                    for m in range(2):
                        t = 2 * j + m
                        dve.wait_ge(R.tile_done, ph.c0 + t + 1)
                        nc.vector.tensor_tensor(x[:, t, :], bank[:, (2 * r + m) % 4, :], x[:, t, :], ALU.add).then_inc(R.tile_free, 1)
                each_slot(dve, ph, slot)

            norm(0)
            for b in range(2):
                dve.wait_ge(split_hi, b + 1)
                nc.vector.tensor_tensor(y_lo[:, 4 * b:4 * b + 4, :], branches[b][:], y_hi[:, 4 * b:4 * b + 4, :].bitcast(F32),
                                        ALU.subtract).then_inc(split_lo, 1)
            each_slot(dve, gates, lambda j, q, r: lo_next(dve, nc, R, gates, j, q, r))
            dve.wait_ge(R.tile_free, gates.end())

            def up_slot(j, q, r):
                lo_next(dve, nc, R, up, j, q, r)
                for m in range(4):
                    t = 4 * j + m
                    dve.wait_ge(R.tile_done, up.c0 + t + 1)
                    nc.vector.tensor_tensor(branch[:, t, :], bank[:, m, :], branch[:, t, :], ALU.mult).then_inc(R.tile_free, 1)
                if j >= 2:
                    for t in range(4 * (j - 2), 4 * (j - 2) + 4):
                        dve.wait_ge(R.tile_free, up.c0 + KT + t + 1)
                        nc.vector.tensor_tensor(branch[:, t, :], branch[:, t, :], branch[:, KT + t, :], ALU.add).then_inc(both, 1)
                    for t in range(4 * (j - 2), 4 * (j - 2) + 4):
                        dve.wait_ge(m_hi, t + 1)
                        nc.vector.tensor_tensor(u_lo[:, t, :], branch[:, t, :], u_hi[:, t, :].bitcast(F32), ALU.subtract).then_inc(m_done, 1)

            each_slot(dve, up, up_slot)
            add_to_x(out)
            norm(1)
            for g in range(GROUPS):
                def relu_slot(j, q, r, g=g):
                    lo_next(dve, nc, R, ff1[g], j, q, r)
                    for m in range(2):
                        t = 2 * j + m
                        a = branch[:, 4 + t % 4, :]
                        dve.wait_ge(R.tile_free, ff1[g].c0 + t + 1)
                        nc.vector.tensor_tensor(branch[:, 12 + t % 4, :], a, a, ALU.mult).then_inc(relu_sq, 1)
                        dve.wait_ge(relu_sq, KT * g + t + 1)
                        dve.wait_ge(relu_hi, KT * g + t + 1)
                        nc.vector.tensor_tensor(y_lo[:, t, :], branch[:, 12 + t % 4, :], y_hi[:, t, :].bitcast(F32),
                                                ALU.subtract).then_inc(relu_done, 1)

                each_slot(dve, ff1[g], relu_slot)
                dve.wait_ge(R.tile_free, ff1[g].end())
                add_to_x(ff2[g])
            dve.wait_ge(p_hi, 1)
            nc.vector.tensor_tensor(y_lo[:, 0:2, :], p_raw[:], y_hi[:, 0:2, :].bitcast(F32), ALU.subtract).then_inc(p_done, 1)

            def ple_slot(j, q, r):
                lo_next(dve, nc, R, ple, j, q, r)
                for t in range(KT):
                    dve.wait_ge(R.tile_done, ple.c0 + t + 1)
                    nc.vector.tensor_copy(branch[:, t, :], bank[:, (8 * r + t) % 4, :]).then_inc(R.tile_free, 1)

            each_slot(dve, ple, ple_slot)
            norm(2)

            def pgate_slot(j, q, r):
                lo_next(dve, nc, R, pgate, j, q, r)
                for m in range(2):
                    t = 2 * j + m
                    dve.wait_ge(R.tile_free, pgate.c0 + t + 1)
                    nc.vector.tensor_tensor(branch[:, t, :], branch[:, t, :], branch[:, 8 + t, :], ALU.mult).then_inc(ple_gated, 1)
                    dve.wait_ge(ple_gated, t + 1)
                    nc.vector.tensor_tensor(x[:, t, :], branch[:, t, :], x[:, t, :], ALU.add).then_inc(x_done, 1)

            each_slot(dve, pgate, pgate_slot)


class Consts:

    def __init__(self, t):
        self.all = t

    def __call__(self, name):
        at, n = CONSTS[name]
        return self.all[:, at:at + n]


def two_layers(nc, io):
    with ExitStack() as ctx:
        C = Consts(ctx.enter_context(nc.sbuf_tensor("consts", [P, N_CONSTS], F32)))
        PV = ctx.enter_context(nc.sbuf_tensor("params", [P, N_PARAMS], F32))
        h = ctx.enter_context(nc.sbuf_tensor("h", [P, KT, L], F32))
        rms = ctx.enter_context(nc.sbuf_tensor("rms", [P, L], F32))
        with nc.cleanup_on_exit():
            mixer_block(nc, io, C, PV, h, rms)
        with nc.cleanup_on_exit():
            ffn_block(nc, io, C, PV, h, rms)
        attn_t = ctx.enter_context(nc.sbuf_tensor("attn_t", [P, 4, GRID], F32))
        rw_t = ctx.enter_context(nc.sbuf_tensor("rw_t", [P, 4, GRID], F32))
        with nc.sbuf_tensor("zr", [P, 14, GRID], F32) as zr:
            with nc.cleanup_on_exit():
                attention_block(nc, io, C, PV, h, zr, attn_t, rms)
            with nc.cleanup_on_exit():
                rwkv_block(nc, io, C, PV, zr, rw_t)
        merge_block(nc, io, C, PV, h, attn_t, rw_t, rms)


def _feature_major(a):
    return np.ascontiguousarray(a.reshape(a.shape[0], -1, P).transpose(2, 1, 0))


def _slots(w, rows=KT, cols=SLOT):
    r, n = w.shape
    assert r == rows * P and n % cols == 0
    return np.ascontiguousarray(w.reshape(rows, P, n // cols, cols).transpose(2, 1, 0, 3).reshape(n // cols, P, rows * cols))


def _columns(*vectors):
    return np.concatenate([np.asarray(v).reshape(-1, P).T for v in vectors], axis=1)


def pack(inputs):
    i = {k: np.asarray(v) for k, v in inputs.items()}
    a = {}
    h = np.concatenate([i["meta_tokens"], i["x"][0]], axis=0)
    a["h"] = _feature_major(h)
    w = i["w_in"][0]
    z = np.pad(w[:, 3072:3104], ((0, 0), (0, SLOT - 32)))
    a["w_in"] = _slots(np.concatenate([w[:, 0:1024], w[:, 1536:2048], w[:, 1024:1536], w[:, 2048:3072], z], axis=1))
    a["w_o"] = _slots(i["w_o"][0])
    wf = i["w_ffn_in"][0]
    pairs = np.concatenate([wf[:, :DFF].reshape(D, FT, 1, P), wf[:, DFF:].reshape(D, FT, 1, P)], axis=2)
    a["w_ffn_in"] = _slots(pairs.reshape(D, 2 * DFF))
    wo = i["w_ffn_out"][0]
    a["w_ffn_out"] = np.concatenate([_slots(np.pad(wo[g * D:(g + 1) * D], ((0, max(0, (g + 1) * D - DFF)), (0, 0)))) for g in range(3)])
    rpb = np.pad(i["na_rel_bias"][0], ((0, 0), (0, 0), (48, 48)))
    a["rpb"] = np.ascontiguousarray(rpb)
    up = np.zeros((33, 512), np.float32)
    up[0:16, 0:256] = i["gla_gate_up_fwd"][0]
    up[16:32, 256:512] = i["gla_gate_up_bwd"][0]
    up[32, 0:256] = i["gla_gate_bias_fwd"][0]
    up[32, 256:512] = i["gla_gate_bias_bwd"][0]
    a["gate_up"] = up
    cw = i["ffn_conv_w"][0]
    a["params"] = np.ascontiguousarray(_columns(
        i["norm_mix_pre"], i["na_out_gain"], i["gla_out_gain"], i["norm_mix_post"], i["norm_ffn_pre"],
        i["norm_ffn_post"], i["ffn_conv_b"], cw[0], cw[1], cw[2],
        i["norm_mix_2"], i["shift_mu_2"], i["w0_2"], i["a0_2"], i["k_k_2"], i["k_a_2"], i["r_k_2"],
        i["lnx_w_2"], i["lnx_b_2"], i["norm_ffn_2"], i["norm_ple_2"]))
    w2 = i["w_in_2"][0]
    q = w2[:, 0:512].reshape(D, 2, 4, HD).transpose(0, 2, 1, 3).reshape(D, 512)
    a["w_in2"] = _slots(np.concatenate([q, w2[:, 512:]], axis=1))
    a["qk_gain"] = np.concatenate([i["q_norm_2"][0], i["k_norm_2"][0]])[None, :]
    a["sink"] = np.ascontiguousarray(i["sink_2"])
    a["lora_w"] = np.ascontiguousarray(i["w2_2"][0])
    a["lora_a"] = np.ascontiguousarray(i["a2_2"][0])
    a["lora_g"] = np.ascontiguousarray(i["g2_2"][0])
    a["w_up"] = np.concatenate([_slots(i["w_up_attn_2"][0], 4, 512), _slots(i["w_up_rwkv_2"][0], 4, 512)])
    a["w_out"] = _slots(i["w_out_2"][0])
    a["w_ff1"] = _slots(i["w_ff1_2"][0])
    a["w_ff2"] = np.concatenate([_slots(i["w_ff2_2"][0][g * D:(g + 1) * D]) for g in range(4)])
    a["w_ple_gate"] = _slots(i["w_ple_gate_2"][0])
    a["w_ple"] = _slots(i["w_ple_2"][0], 2, 1024)
    a["p"] = _feature_major(i["p_2"][0, 0])
    a["consts"], a["consts2"], a["levels"] = shape_constants()
    return a


def kernel(**inputs):
    import concourse.bacc as _bacc
    from concourse import mybir as _mybir
    from concourse.bass_utils import run_bass_kernel_spmd as _run

    nc = _bacc.Bacc("TRN2", target_bir_lowering=False, num_devices=1)
    arrays, io = {}, {}
    for name, value in pack(inputs).items():
        arrays[f"in_{name}"] = value
        io[name] = nc.dram_tensor(f"in_{name}", value.shape, _mybir.dt.from_np(value.dtype), kind="ExternalInput").ap()
    io["out"] = nc.dram_tensor("out_0", (P, KT, GRID), _mybir.dt.float32, kind="ExternalOutput").ap()
    two_layers(nc, io)
    r = _run(nc, [arrays], core_ids=[0])
    out = r.results[0]["out_0"]
    return np.ascontiguousarray(out.transpose(2, 1, 0).reshape(1, GRID, D))
```
